# Optimizing a Trainium2 kernel written in Bass

```python
import math
import jax, jax.numpy as jnp
from jax import lax
import numpy as np

D_MODEL = 1024
BATCH = 1
SEQ = 512
DEPTH = 2

N_MIXERS = 2
RMS_EPS = 1e-6
ROPE_THETA = 10000.0
Q_BLOCK = 128
MAX_POS_OFFSET = 4096

DA_HEADS = 8
DA_QK_DIM = 64
DA_V_DIM = 2 * DA_QK_DIM
DA_WIDTH = DA_HEADS * DA_V_DIM

MLA_HEADS = 8
MLA_Q_LORA = 384
MLA_KV_LORA = 256
MLA_NOPE = 128
MLA_ROPE = 64
MLA_V = 128
MLA_WIDTH = MLA_HEADS * MLA_V
MLA_IN = MLA_Q_LORA + MLA_KV_LORA + MLA_ROPE + MLA_WIDTH


def _rmsnorm(x, g):
    xf = x.astype(jnp.float32)
    y = xf * lax.rsqrt(jnp.mean(xf * xf, axis=-1, keepdims=True) + RMS_EPS)
    return (y * g.astype(jnp.float32)).astype(x.dtype)

def _rope(x, positions):
    d = x.shape[-1]
    half = d // 2
    inv = ROPE_THETA ** (-jnp.arange(half, dtype=jnp.float32) / half)
    ang = positions.astype(jnp.float32)[..., None] * inv
    cos = jnp.cos(ang)[:, :, None, :]
    sin = jnp.sin(ang)[:, :, None, :]
    xf = x.astype(jnp.float32)
    x1, x2 = xf[..., :half], xf[..., half:]
    out = jnp.concatenate([x1 * cos - x2 * sin, x2 * cos + x1 * sin], axis=-1)
    return out.astype(x.dtype)

def _to_blocks(t):
    b, s = t.shape[:2]
    t = t.reshape((b, s // Q_BLOCK, Q_BLOCK) + t.shape[2:])
    return jnp.moveaxis(t, 1, 0)

def _from_blocks(t):
    t = jnp.moveaxis(t, 0, 1)
    return t.reshape((t.shape[0], t.shape[1] * t.shape[2]) + t.shape[3:])

def _lambda_init(layer_idx):
    return 0.8 - 0.6 * math.exp(-0.3 * layer_idx)

def _modulation(c, ada_w, ada_b):
    mod = jax.nn.silu(c) @ ada_w + ada_b
    shift, scale, gate = jnp.split(mod[:, None, :], 3, axis=-1)
    return shift, scale, gate

def _diff_attention(h, positions, w_in, lam_q1, lam_k1, lam_q2, lam_k2, subln_g, w_out, lambda_init):
    b, s, _ = h.shape
    proj = h @ w_in
    q, k, v, z = jnp.split(proj, [DA_WIDTH, 2 * DA_WIDTH, 3 * DA_WIDTH], axis=-1)
    q = _rope(q.reshape(b, s, 2 * DA_HEADS, DA_QK_DIM), positions)
    k = _rope(k.reshape(b, s, 2 * DA_HEADS, DA_QK_DIM), positions)
    q = q.reshape(b, s, DA_HEADS, 2, DA_QK_DIM)
    k = k.reshape(b, s, DA_HEADS, 2, DA_QK_DIM)
    v = v.reshape(b, s, DA_HEADS, DA_V_DIM)
    f32 = jnp.float32
    lam = (jnp.exp(jnp.sum(lam_q1.astype(f32) * lam_k1.astype(f32)))
           - jnp.exp(jnp.sum(lam_q2.astype(f32) * lam_k2.astype(f32))) + lambda_init)
    scale = DA_QK_DIM ** -0.5

    def block(qb):
        sc = jnp.einsum('bqhcd,bkhcd->bhcqk', qb, k, preferred_element_type=f32) * scale
        p = jax.nn.softmax(sc, axis=-1)
        p = p[:, :, 0] - lam * p[:, :, 1]
        return jnp.einsum('bhqk,bkhd->bqhd', p.astype(v.dtype), v)

    o = _from_blocks(lax.map(block, _to_blocks(q)))
    o = _rmsnorm(o, subln_g) * (1.0 - lambda_init)
    o = o.reshape(b, s, DA_WIDTH) * jax.nn.silu(z)
    return o @ w_out

def _mla(h, positions, w_in, q_a_norm_g, w_q_b, kv_a_norm_g, w_kv_b, w_out):
    b, s, _ = h.shape
    proj = h @ w_in
    q_a, c_kv, k_pe, z = jnp.split(
        proj, [MLA_Q_LORA, MLA_Q_LORA + MLA_KV_LORA, MLA_Q_LORA + MLA_KV_LORA + MLA_ROPE], axis=-1)
    q = (_rmsnorm(q_a, q_a_norm_g) @ w_q_b).reshape(b, s, MLA_HEADS, MLA_NOPE + MLA_ROPE)
    q_nope = q[..., :MLA_NOPE]
    q_pe = _rope(q[..., MLA_NOPE:], positions)
    k_pe = _rope(k_pe[:, :, None, :], positions)[:, :, 0]
    kv = (_rmsnorm(c_kv, kv_a_norm_g) @ w_kv_b).reshape(b, s, MLA_HEADS, MLA_NOPE + MLA_V)
    k_nope, v = kv[..., :MLA_NOPE], kv[..., MLA_NOPE:]
    scale = (MLA_NOPE + MLA_ROPE) ** -0.5
    f32 = jnp.float32

    def block(args):
        qn, qp = args
        sc = (jnp.einsum('bqhd,bkhd->bhqk', qn, k_nope, preferred_element_type=f32)
              + jnp.einsum('bqhr,bkr->bhqk', qp, k_pe, preferred_element_type=f32)) * scale
        p = jax.nn.softmax(sc, axis=-1)
        return jnp.einsum('bhqk,bkhd->bqhd', p.astype(v.dtype), v)

    o = _from_blocks(lax.map(block, (_to_blocks(q_nope), _to_blocks(q_pe))))
    o = o.reshape(b, s, MLA_WIDTH) * jax.nn.silu(z)
    return o @ w_out

def first_inputs(seed: int = 0) -> dict:
    key = jax.random.key(seed)
    ks = jax.random.split(key, 24)
    f32 = jnp.float32
    nrm = lambda k, shape, fan_in: jax.random.normal(k, shape, f32) * (fan_in ** -0.5)
    gain = lambda k, n: 1.0 + 0.02 * jax.random.normal(k, (n,), f32)
    D = D_MODEL
    x = jax.random.normal(ks[0], (BATCH, SEQ, D), f32)
    c = jax.random.normal(ks[1], (BATCH, D), f32)
    offs = jax.random.randint(ks[2], (BATCH, 1), 0, MAX_POS_OFFSET, dtype=jnp.int32)
    positions = offs + jnp.arange(SEQ, dtype=jnp.int32)[None, :]
    return {
        "x": x,
        "c": c,
        "positions": positions,
        "ada_w0": nrm(ks[3], (D, 3 * D), D),
        "ada_b0": 0.02 * jax.random.normal(ks[4], (3 * D,), f32),
        "norm_g0": gain(ks[5], D),
        "w_in0": nrm(ks[6], (D, 4 * DA_WIDTH), D),
        "lam_q1": 0.1 * jax.random.normal(ks[7], (DA_QK_DIM,), f32),
        "lam_k1": 0.1 * jax.random.normal(ks[8], (DA_QK_DIM,), f32),
        "lam_q2": 0.1 * jax.random.normal(ks[9], (DA_QK_DIM,), f32),
        "lam_k2": 0.1 * jax.random.normal(ks[10], (DA_QK_DIM,), f32),
        "subln_g": gain(ks[11], DA_V_DIM),
        "w_out0": nrm(ks[12], (DA_WIDTH, D), DA_WIDTH),
        "ada_w1": nrm(ks[13], (D, 3 * D), D),
        "ada_b1": 0.02 * jax.random.normal(ks[14], (3 * D,), f32),
        "norm_g1": gain(ks[15], D),
        "w_in1": nrm(ks[16], (D, MLA_IN), D),
        "q_a_norm_g": gain(ks[17], MLA_Q_LORA),
        "w_q_b": nrm(ks[18], (MLA_Q_LORA, MLA_HEADS * (MLA_NOPE + MLA_ROPE)), MLA_Q_LORA),
        "kv_a_norm_g": gain(ks[19], MLA_KV_LORA),
        "w_kv_b": nrm(ks[20], (MLA_KV_LORA, MLA_HEADS * (MLA_NOPE + MLA_V)), MLA_KV_LORA),
        "w_out1": nrm(ks[21], (MLA_WIDTH, D), MLA_WIDTH),
        "final_norm_g": gain(ks[22], D),
    }

def first_block(x, c, positions,
              ada_w0, ada_b0, norm_g0, w_in0, lam_q1, lam_k1, lam_q2, lam_k2, subln_g, w_out0,
              ada_w1, ada_b1, norm_g1, w_in1, q_a_norm_g, w_q_b, kv_a_norm_g, w_kv_b, w_out1,
              final_norm_g):
    ada_w = (ada_w0, ada_w1)
    ada_b = (ada_b0, ada_b1)
    norm_g = (norm_g0, norm_g1)
    for i in range(DEPTH):
        shift, scale, gate = _modulation(c, ada_w[i], ada_b[i])
        h = _rmsnorm(x, norm_g[i]) * (1.0 + scale) + shift
        if i % N_MIXERS == 0:
            y = _diff_attention(h, positions, w_in0, lam_q1, lam_k1, lam_q2, lam_k2,
                                subln_g, w_out0, _lambda_init(i))
        else:
            y = _mla(h, positions, w_in1, q_a_norm_g, w_q_b, kv_a_norm_g, w_kv_b, w_out1)
        x = x + gate * y
    return _rmsnorm(x, final_norm_g)


DEPTH_2 = 1

D_MIX = D_MODEL
HEAD_DIM = 64
D_ATTN = D_MIX // 2
N_HEADS = D_ATTN // HEAD_DIM
D_CONV = D_MIX - D_ATTN
D_IN = 3 * D_ATTN + 2 * D_CONV
CONV_WIDTH = 31
DILATED_BRANCHES = ((128, 1), (512, 4), (2048, 16))
ATTN_BLOCK = 128
N_GROUPS = 4
EXPERTS_PER_GROUP = 8
N_EXPERTS = N_GROUPS * EXPERTS_PER_GROUP
TOP_K_INNER = 2
D_EXPERT = D_MODEL // 2
MOE_BLOCK = 256
NORM_EPS = 1e-6
N_MOD = 6


def rms_norm(x, g):
    x32 = x.astype(jnp.float32)
    y = x32 * lax.rsqrt(jnp.mean(x32 * x32, axis=-1, keepdims=True) + NORM_EPS)
    return (y * g.astype(jnp.float32)).astype(x.dtype)

def layer_norm(x, g, b):
    x32 = x.astype(jnp.float32)
    mu = jnp.mean(x32, axis=-1, keepdims=True)
    var = jnp.mean(jnp.square(x32 - mu), axis=-1, keepdims=True)
    y = (x32 - mu) * lax.rsqrt(var + NORM_EPS)
    return (y * g.astype(jnp.float32) + b.astype(jnp.float32)).astype(x.dtype)

def alibi_slopes(n_heads):
    return jnp.asarray(2.0 ** (-8.0 * np.arange(1, n_heads + 1) / n_heads), dtype=jnp.float32)

def dilated_branch(q, k, v, slopes, window, dil):
    B, H, S, Dh = q.shape
    L = S // dil
    n_back = window // dil
    nb = -(-L // ATTN_BLOCK)
    Lp = nb * ATTN_BLOCK

    def to_blocks(t):
        t = t.reshape(B, H, L, dil, Dh).transpose(0, 1, 3, 2, 4)
        t = jnp.pad(t, ((0, 0), (0, 0), (0, 0), (0, Lp - L), (0, 0)))
        return t.reshape(B, H, dil, nb, ATTN_BLOCK, Dh)

    def with_prev(t):
        prev = jnp.pad(t[:, :, :, :-1], ((0, 0), (0, 0), (0, 0), (1, 0), (0, 0), (0, 0)))
        return jnp.concatenate([prev, t], axis=4)

    qb = to_blocks(q)
    kc = with_prev(to_blocks(k))
    vc = with_prev(to_blocks(v))
    s = jnp.einsum('bhrnqd,bhrnkd->bhrnqk', qb, kc,
                   preferred_element_type=jnp.float32) * (HEAD_DIM ** -0.5)
    qi = np.arange(ATTN_BLOCK)[:, None] + ATTN_BLOCK
    ki = np.arange(2 * ATTN_BLOCK)[None, :]
    delta = qi - ki
    blk_ok = (np.arange(nb)[:, None, None] > 0) | (ki[None] >= ATTN_BLOCK)
    valid = (delta >= 0) & (delta <= n_back) & blk_ok
    bias = -slopes[:, None, None] * jnp.asarray(delta * dil, dtype=jnp.float32)
    s = s + bias[None, :, None, None]
    s = jnp.where(valid[None, None, None], s, -jnp.inf)
    m = jnp.max(s, axis=-1)
    p = jnp.exp(s - m[..., None])
    l = jnp.sum(p, axis=-1)
    o = jnp.einsum('bhrnqk,bhrnkd->bhrnqd', p, vc.astype(jnp.float32))

    def from_blocks(t, trailing):
        t = t.reshape((B, H, dil, Lp) + trailing)[:, :, :, :L]
        t = jnp.moveaxis(t, 2, 3)
        return t.reshape((B, H, S) + trailing)

    return from_blocks(o, (Dh,)), from_blocks(m, ()), from_blocks(l, ())

def dilated_attention(q, k, v, slopes):
    outs = [dilated_branch(q, k, v, slopes, w, d) for (w, d) in DILATED_BRANCHES]
    m_all = jnp.stack([m for (_, m, _) in outs])
    m_max = jnp.max(m_all, axis=0)
    num = 0.0
    den = 0.0
    for (o, m, l) in outs:
        a = jnp.exp(m - m_max)
        num = num + a[..., None] * o
        den = den + a * l
    return num / den[..., None]

def conformer_conv(a, b, conv_w, conv_b, ln_g, ln_b):
    u = a * jax.nn.sigmoid(b)
    y = lax.conv_general_dilated(u, conv_w[:, None, :].astype(u.dtype), window_strides=(1,),
                                 padding=[(CONV_WIDTH - 1, 0)],
                                 dimension_numbers=('NWC', 'WIO', 'NWC'),
                                 feature_group_count=D_CONV) + conv_b
    return jax.nn.silu(layer_norm(y, ln_g, ln_b))

def hier_moe(h, w_rg, b_rg, w_re, b_re, w_gate, w_up, w_down):
    B, S, D = h.shape
    T = B * S
    hf = h.reshape(T, D)
    tix = jnp.arange(T)
    g_logits = (hf @ w_rg + b_rg).astype(jnp.float32)
    g_prob = jax.nn.softmax(g_logits, axis=-1)
    grp = jnp.argmax(g_logits, axis=-1)
    p_grp = g_prob[tix, grp]
    e_logits = (hf @ w_re + b_re).astype(jnp.float32).reshape(T, N_GROUPS, EXPERTS_PER_GROUP)
    e_logits = e_logits[tix, grp]
    top_val, top_idx = lax.top_k(e_logits, TOP_K_INNER)
    top_w = jax.nn.softmax(top_val, axis=-1) * p_grp[:, None]

    A = T * TOP_K_INNER
    eid = (grp[:, None] * EXPERTS_PER_GROUP + top_idx).reshape(A).astype(jnp.int32)
    tok = jnp.repeat(tix, TOP_K_INNER).astype(jnp.int32)
    wts = top_w.reshape(A)
    order = jnp.argsort(eid)
    s_eid, s_tok, s_w = eid[order], tok[order], wts[order]
    counts = jnp.bincount(eid, length=N_EXPERTS)
    start = jnp.cumsum(counts) - counts
    padded = ((counts + MOE_BLOCK - 1) // MOE_BLOCK) * MOE_BLOCK
    pad_end = jnp.cumsum(padded)
    pad_start = pad_end - padded
    dest = pad_start[s_eid] + (jnp.arange(A) - start[s_eid])
    P = (-(-A // MOE_BLOCK)) * MOE_BLOCK + N_EXPERTS * MOE_BLOCK
    nblk = P // MOE_BLOCK
    buf_tok = jnp.full((P,), T, dtype=jnp.int32).at[dest].set(s_tok)
    buf_w = jnp.zeros((P,), dtype=jnp.float32).at[dest].set(s_w)
    blk_eid = jnp.clip(jnp.searchsorted(pad_end, jnp.arange(nblk) * MOE_BLOCK, side='right'),
                       0, N_EXPERTS - 1)
    x_pad = jnp.concatenate([hf, jnp.zeros((1, D), hf.dtype)], axis=0)
    xb = x_pad[buf_tok].reshape(nblk, MOE_BLOCK, D)

    def expert_block(args):
        xblk, e = args
        return (jax.nn.silu(xblk @ w_gate[e]) * (xblk @ w_up[e])) @ w_down[e]

    yb = lax.map(expert_block, (xb, blk_eid)).reshape(P, D)
    out = jnp.zeros((T + 1, D), yb.dtype).at[buf_tok].add(yb * buf_w[:, None].astype(yb.dtype))[:T]
    return out.reshape(B, S, D).astype(h.dtype)

def second_inputs(seed: int = 0) -> dict:
    key = jax.random.key(seed)
    ks = jax.random.split(key, 24)
    f32 = jnp.float32
    nrm = lambda k, shape, s: jax.random.normal(k, shape, f32) * s
    L = DEPTH_2
    return {
        "x": nrm(ks[0], (BATCH, SEQ, D_MODEL), 1.0),
        "c": nrm(ks[1], (BATCH, D_MODEL), 1.0),
        "w_mod": nrm(ks[2], (L, D_MODEL, N_MOD * D_MODEL), 0.5 * D_MODEL ** -0.5),
        "b_mod": nrm(ks[3], (L, N_MOD * D_MODEL), 0.01),
        "g_norm1": 1.0 + nrm(ks[4], (L, D_MODEL), 0.02),
        "w_in": nrm(ks[5], (L, D_MODEL, D_IN), D_MODEL ** -0.5),
        "conv_w": nrm(ks[6], (L, CONV_WIDTH, D_CONV), CONV_WIDTH ** -0.5),
        "conv_b": nrm(ks[7], (L, D_CONV), 0.01),
        "conv_ln_g": 1.0 + nrm(ks[8], (L, D_CONV), 0.02),
        "conv_ln_b": nrm(ks[9], (L, D_CONV), 0.01),
        "w_out": nrm(ks[10], (L, D_MIX, D_MODEL), D_MIX ** -0.5),
        "g_norm2": 1.0 + nrm(ks[11], (L, D_MODEL), 0.02),
        "w_router_group": nrm(ks[12], (L, D_MODEL, N_GROUPS), D_MODEL ** -0.5),
        "b_router_group": nrm(ks[13], (L, N_GROUPS), 0.01),
        "w_router_expert": nrm(ks[14], (L, D_MODEL, N_EXPERTS), D_MODEL ** -0.5),
        "b_router_expert": nrm(ks[15], (L, N_EXPERTS), 0.01),
        "w_exp_gate": nrm(ks[16], (L, N_EXPERTS, D_MODEL, D_EXPERT), D_MODEL ** -0.5),
        "w_exp_up": nrm(ks[17], (L, N_EXPERTS, D_MODEL, D_EXPERT), D_MODEL ** -0.5),
        "w_exp_down": nrm(ks[18], (L, N_EXPERTS, D_EXPERT, D_MODEL), D_EXPERT ** -0.5),
        "g_final": 1.0 + nrm(ks[19], (D_MODEL,), 0.02),
    }

def second_block(x, c, w_mod, b_mod, g_norm1, w_in, conv_w, conv_b, conv_ln_g, conv_ln_b, w_out,
              g_norm2, w_router_group, b_router_group, w_router_expert, b_router_expert,
              w_exp_gate, w_exp_up, w_exp_down, g_final):
    B, S, D = x.shape
    slopes = alibi_slopes(N_HEADS)
    c_act = jax.nn.silu(c)

    def split_heads(t):
        return t.reshape(B, S, N_HEADS, HEAD_DIM).transpose(0, 2, 1, 3)

    for l in range(DEPTH_2):
        mod = c_act @ w_mod[l] + b_mod[l]
        sh1, sc1, gt1, sh2, sc2, gt2 = jnp.split(mod[:, None, :], N_MOD, axis=-1)

        h = rms_norm(x, g_norm1[l]) * (1.0 + sc1) + sh1
        u = h @ w_in[l]
        q, k, v, ga, gb = jnp.split(
            u, [D_ATTN, 2 * D_ATTN, 3 * D_ATTN, 3 * D_ATTN + D_CONV], axis=-1)
        attn = dilated_attention(split_heads(q), split_heads(k), split_heads(v), slopes)
        attn = attn.transpose(0, 2, 1, 3).reshape(B, S, D_ATTN).astype(x.dtype)
        conv = conformer_conv(ga, gb, conv_w[l], conv_b[l], conv_ln_g[l], conv_ln_b[l])
        mix = jnp.concatenate([attn, conv], axis=-1) @ w_out[l]
        x = x + gt1 * mix

        h2 = rms_norm(x, g_norm2[l]) * (1.0 + sc2) + sh2
        x = x + gt2 * hier_moe(h2, w_router_group[l], b_router_group[l], w_router_expert[l],
                               b_router_expert[l], w_exp_gate[l], w_exp_up[l], w_exp_down[l])

    return rms_norm(x, g_final)


def setup_inputs(seed=0):
    out = dict(first_inputs(seed))
    for name, value in second_inputs(seed + 1).items():
        if name != "x":
            out[name + "_2"] = value
    return out


def reference(
    x, c, positions, ada_w0, ada_b0, norm_g0, w_in0, lam_q1, lam_k1, lam_q2, lam_k2, subln_g,
    w_out0, ada_w1, ada_b1, norm_g1, w_in1, q_a_norm_g, w_q_b, kv_a_norm_g, w_kv_b, w_out1,
    final_norm_g, c_2, w_mod_2, b_mod_2, g_norm1_2, w_in_2, conv_w_2, conv_b_2, conv_ln_g_2,
    conv_ln_b_2, w_out_2, g_norm2_2, w_router_group_2, b_router_group_2, w_router_expert_2,
    b_router_expert_2, w_exp_gate_2, w_exp_up_2, w_exp_down_2, g_final_2,
):
    x = first_block(
        x, c, positions, ada_w0, ada_b0, norm_g0, w_in0, lam_q1, lam_k1, lam_q2, lam_k2,
        subln_g, w_out0, ada_w1, ada_b1, norm_g1, w_in1, q_a_norm_g, w_q_b, kv_a_norm_g, w_kv_b,
        w_out1, final_norm_g,
    )
    return second_block(
        x, c_2, w_mod_2, b_mod_2, g_norm1_2, w_in_2, conv_w_2, conv_b_2, conv_ln_g_2,
        conv_ln_b_2, w_out_2, g_norm2_2, w_router_group_2, b_router_group_2, w_router_expert_2,
        b_router_expert_2, w_exp_gate_2, w_exp_up_2, w_exp_down_2, g_final_2,
    )


_drawn_inputs = setup_inputs


def setup_inputs(seed=0):
    import zlib

    import numpy as np

    out = dict(_drawn_inputs(seed))
    spreads = {}
    factors = {'norm_g0': 4.371,
     'lam_q1': 4.156,
     'lam_k1': 5.876,
     'lam_q2': 8.0,
     'lam_k2': 8.0,
     'subln_g': 5.071,
     'ada_b1': 3.972,
     'norm_g1': 7.307,
     'q_a_norm_g': 8.0,
     'kv_a_norm_g': 6.588,
     'b_mod_2': 4.143,
     'g_norm1_2': 8.0,
     'conv_b_2': 8.0,
     'conv_ln_g_2': 8.0,
     'conv_ln_b_2': 8.0,
     'g_norm2_2': 4.768,
     'b_router_group_2': 5.712,
     'b_router_expert_2': 8.0}
    for name, (base, spread) in spreads.items():
        noise = np.random.default_rng([zlib.crc32(name.encode()), seed]).standard_normal(out[name].shape)
        drawn = base * np.exp(spread * noise) if base else spread * noise
        out[name] = __import__('jax').numpy.asarray(drawn.astype(out[name].dtype))
    for name, factor in factors.items():
        out[name] = (out[name] * factor).astype(out[name].dtype)
    return out
```

```python
import math
from contextlib import ExitStack

import numpy as np

import concourse.bass as bass
from concourse import mybir

F32 = mybir.dt.float32
I32 = mybir.dt.int32
ALU = mybir.AluOpType
ACT = mybir.ActivationFunctionType
AX = mybir.AxisListType

P = 128
T = 512
TT = T // P
D = 1024
KT = D // P
W = 512
EPS = 1e-6
HEADS = 8
NEG = -1e30

DA_DIM = 64
LAMBDA_INIT = 0.8 - 0.6 * math.exp(-0.3 * 0)
Q_LORA, KV_LORA, NOPE, ROPE, MLA_V = 384, 256, 128, 64, 128
MLA_SCALE = (NOPE + ROPE) ** -0.5
ALIBI_DIM = 64
TAPS = 31
PAD = TAPS - 1
CH = 4

GROUPS, PER_GROUP = 4, 8
EXPERTS = GROUPS * PER_GROUP
FF = 512
FT = FF // P
SLOTS = 128
MORE = T // SLOTS - 1
OVER = 2 * T // SLOTS
ITEMS = EXPERTS + OVER

R1 = dict(ada_b0=0, norm_g0=24, ada_b1=32, norm_g1=56, b_mod=64, g_norm1=112)
R1_ROWS = 120
R2 = dict(g_norm2=0, qa_g=8, kv_g=11, conv_b=13, ln_g=17, ln_b=21, c=25, c_2=33, subln_g=41)
R2_ROWS = 42
R3_ROWS = TAPS * CH
SOURCES = dict(ada_b0="ada_b0", norm_g0="norm_g0", ada_b1="ada_b1", norm_g1="norm_g1", b_mod="b_mod_2",
               g_norm1="g_norm1_2", g_norm2="g_norm2_2", qa_g="q_a_norm_g", kv_g="kv_a_norm_g", conv_b="conv_b_2",
               ln_g="conv_ln_g_2", ln_b="conv_ln_b_2", c="c", c_2="c_2", subln_g="subln_g")
K_IDENT, K_ROT, K_UPPER, K_ONES, K_INV = 0, 128, 256, 384, 512
K_IOTA4, K_IOTA32, K_ITEM = 513, 517, 549
K_COLS = 549 + OVER

TWO_PI = 2 * math.pi
PI_A = 6.28125
PI_B = float(np.float32(np.round((TWO_PI - PI_A) * 2 ** 22) / 2 ** 22))
PI_C = TWO_PI - PI_A - PI_B
ROUNDER = 12582912.0
PI_BELOW = 3.1415925


class Banks:

    def __init__(self, banks, filled, freed):
        self.banks, self.filled, self.freed, self.n = banks, filled, freed, 0

    def claim(self, pe):
        if self.n >= len(self.banks):
            pe.wait_ge(self.freed, self.n - len(self.banks) + 1)
        self.n += 1
        return self.banks[(self.n - 1) % len(self.banks)]

    def take(self, eng):
        self.n += 1
        eng.wait_ge(self.filled, self.n)
        return self.banks[(self.n - 1) % len(self.banks)]


class Steps:

    def __init__(self, eng, sem):
        self.eng, self.sem, self.n = eng, sem, 0

    def __call__(self, ins):
        ins.then_inc(self.sem, 1)
        self.n += 1
        return self.n

    def settle(self, n=None):
        n = self.n if n is None else n
        if n > 0:
            self.eng.wait_ge(self.sem, n)


def dense_stream():
    units = [("ada0", u) for u in range(4)] + [("win0", u) for u in range(8)]
    units += [("ada0", u) for u in (4, 5)] + [("wout0", u) for u in range(2)]
    units += [("ada1", u) for u in range(4)] + [("win1", u) for u in range(4)]
    units += [("wqb", u) for u in range(2)] + [("wkvb", 0)]
    units += [("ada1", u) for u in (4, 5)] + [("wout1", u) for u in range(2)]
    units += [("mod2", u) for u in range(4)] + [("win2", u) for u in (3, 4, 0, 1, 2)]
    units += [("mod2", u) for u in (4, 5)] + [("wout2", u) for u in range(2)]
    units += [("mod2", u) for u in range(6, 12)]
    return units


def fused_kernel(nc, a, out, xs, ys):
    with ExitStack() as ctx:
        def sb(name, shape, dt=F32):
            return ctx.enter_context(nc.sbuf_tensor(name, shape, dt))

        def sem(name):
            return ctx.enter_context(nc.semaphore(name))

        RING = 4
        ring = [sb(f"ring{i}", [P, 4096]) for i in range(RING)]
        x = sb("x", [P, TT, D])
        hT = sb("hT", [P, 8, T])
        bufA = sb("bufA", [P, 4096])
        bufB = sb("bufB", [P, 4096])
        bufC = sb("bufC", [P, 4096])
        bufD = sb("bufD", [P, 4096])
        bufE = sb("bufE", [P, 2560])
        k_sb = sb("k_sb", [P, K_COLS])
        cosT = sb("cosT", [P, T])
        sinT = sb("sinT", [P, T])
        gate_row = sb("gate_row", [P, D])
        norm_row = sb("norm_row", [P, D])
        probs = sb("probs", [P, 4, W])
        mix = sb("mix", [P, 3, W])
        probsT = sb("probsT", [P, 2, W])
        col1 = sb("col1", [P, R1_ROWS])
        col2 = sb("col2", [P, R2_ROWS])
        col3 = sb("col3", [P, R3_ROWS])
        w_router = sb("w_router", [P, KT, GROUPS + EXPERTS])
        b_router = sb("b_router", [P, GROUPS + EXPERTS])
        zero = sb("zero", [P, 128])
        silu_c = sb("silu_c", [P, 16])
        mods = sb("mods", [P, 16])
        aff = sb("aff", [P, 8])
        ss = sb("ss", [P, 16])
        pw = sb("pw", [P, 4, 16])
        half_neg = sb("half_neg", [P, 16])
        negmax = sb("negmax", [P, 64])
        sums = sb("sums", [P, 64])
        inv_sums = sb("inv_sums", [P, 64])
        lam = sb("lam", [P, 4])
        dest = sb("dest", [P, 2, TT], I32)
        over_ids = sb("over_ids", [P, OVER + 1], I32)
        wts = sb("wts", [P, 2, TT])
        tiny = sb("tiny", [P, 16])
        shift2 = sb("shift2", [P, 8])

        psum = [ctx.enter_context(nc.psum_tensor(f"bank{i}", [P, W], F32)) for i in range(8)]

        ident = k_sb[:, K_IDENT:K_IDENT + P]
        rot = k_sb[:, K_ROT:K_ROT + P]
        upper = k_sb[:, K_UPPER:K_UPPER + P]
        ones = k_sb[:, K_ONES:K_ONES + P]

        def tok(buf, n=D, lo=0):
            return buf[:, lo:lo + TT * n].rearrange("p (t n) -> p t n", t=TT)

        def feat(buf, blocks=8, lo=0):
            return buf[:, lo:lo + blocks * T].rearrange("p (b n) -> p b n", b=blocks)

        A8, B8 = feat(bufA), feat(bufB)
        C_tok, D_tok = tok(bufC), tok(bufD)
        o_raw = hT[:, :, :].rearrange("p b n -> p (b n)").rearrange("p (t n) -> p t n", t=TT)

        gate_cols = bufE[:, 0:D].rearrange("p (j c) -> p j c", j=8)

        at = [0]

        def route_buf(*shape):
            n = math.prod(shape)
            view = bufE[:, at[0]:at[0] + n]
            at[0] += n
            return view if len(shape) == 1 else view.rearrange("p (a b) -> p a b", a=shape[0])

        NE = EXPERTS
        logits, by_e = route_buf(TT, GROUPS + NE), [route_buf(TT, NE) for _ in range(6)]
        masked, hit, cand, first_hot, second_hot, mask_v = by_e
        rank_v = route_buf(TT + 1, NE)
        rt_gexp, g_hit, g_hot = (route_buf(TT, GROUPS) for _ in range(3))
        by_t = [route_buf(TT) for _ in range(14)]
        rt_d = by_t[0]
        more, more_incl, more_tmp, more_before = (route_buf(NE) for _ in range(4))
        item_cmp = route_buf(OVER, NE)
        over_f = route_buf(OVER + 1)
        first_idx, second_idx = by_t[1], by_t[2]

        def inputs_list():
            loads = [(k_sb[:, :], a["constants"])]
            rows = lambda name: (a[name][0] if len(a[name].shape) == 2 else a[name]).rearrange("(r c) -> r c", c=P)
            for at_col, table in ((0, R1), (P, R2)):
                for name, r in table.items():
                    src = rows(SOURCES[name])
                    loads.append((bufD[r:r + src.shape[0], at_col:at_col + P], src))
            loads.append((bufD[0:R3_ROWS, 2 * P:3 * P], a["conv_w_2"][0].rearrange("t (c n) -> (t c) n", n=P)))
            for n, name in enumerate(("lam_q1", "lam_k1", "lam_q2", "lam_k2")):
                lo = 3 * P + n * DA_DIM
                loads.append((bufD[:, lo:lo + DA_DIM], a[name].unsqueeze(0).to_broadcast([P, DA_DIM])))
            loads.append((bufE[:, 0:T].bitcast(I32), a["positions"].to_broadcast([P, T])))
            loads.append((w_router[:, :, 0:GROUPS], a["w_router_group_2"][0].rearrange("(k p) n -> p k n", p=P)))
            loads.append((w_router[:, :, GROUPS:], a["w_router_expert_2"][0].rearrange("(k p) n -> p k n", p=P)))
            loads.append((b_router[:, 0:GROUPS], a["b_router_group_2"].to_broadcast([P, GROUPS])))
            loads.append((b_router[:, GROUPS:], a["b_router_expert_2"].to_broadcast([P, NE])))
            return loads

        in_loads = inputs_list()
        N_IN = len(in_loads)

        s_in = sem("inputs_loaded")
        s_xin = sem("x_loaded")
        w_in = [sem(f"unit_loaded{i}") for i in range(RING)]
        unit_used = sem("unit_used")
        act_filled, act_freed = sem("act_bank_filled"), sem("act_bank_freed")
        tr_filled, tr_freed = sem("transposed_bank_filled"), sem("transposed_bank_freed")
        dve_filled, dve_freed = sem("dve_bank_filled"), sem("dve_bank_freed")
        act_step, dve_step, pool_step = sem("act_step"), sem("dve_step"), sem("pool_step")
        silu_ready = sem("silu_c_ready")
        lam_dots, lam_exps = sem("lambda_dots_ready"), sem("lambda_exps_ready")
        angles_ready, sincos_ready = sem("angles_ready"), sem("sincos_ready")
        squares_ready, rstd_ready = sem("squares_ready"), sem("rstd_ready")
        xn_ready, x_ready = sem("xn_ready"), sem("x_ready")
        aff_ready = sem("affine_ready")
        hT_act, hT_dve = sem("hT_by_act"), sem("hT_by_dve")
        raw_ready, rope_ready = sem("raw_ready"), sem("rope_ready")
        v_ready, z_ready = sem("v_ready"), sem("z_ready")
        max_ready, exp_ready, mix_ready = sem("max_ready"), sem("exp_ready"), sem("mix_ready")
        og_ready, oT_ready = sem("gated_output_ready"), sem("outputT_ready")
        gatecols_ready, gate_ready = sem("gate_columns_ready"), sem("gate_row_ready")
        raw1_ready, n1_ready, nT_ready = sem("latents_ready"), sem("latents_normed"), sem("latentsT_ready")
        qk_ready = sem("qk_ready")
        norm_row_in, norm_row_used = sem("norm_row_loaded"), sem("norm_row_used")
        alibi_in = sem("alibi_loaded")
        sig_ready, u_used = sem("sigmoid_ready"), sem("sigmoid_used")
        conv_ready, ln_ready, ln_sq = sem("conv_ready"), sem("layernorm_ready"), sem("ln_squares_ready")
        zero_ready, zeros_out = sem("zero_ready"), sem("zeros_stored")
        gexp_in, gexp_out = sem("router_exp_in"), sem("router_exp_out")
        mask_ready, dest_ready = sem("mask_ready"), sem("dest_ready")
        rows_out = sem("rows_scattered")
        over_ready = sem("further_items_ready")
        e_in = [[sem(f"expert_{n}_loaded{p}") for n in ("gate", "up", "down")] for p in range(2)]
        xg_in = [sem(f"rows_loaded{p}") for p in range(2)]
        xg_read = sem("rows_transposed")
        xgT_ready = sem("rowsT_ready")
        gate_done, up_done, down_done = sem("gate_done"), sem("up_done"), sem("down_done")
        sg_ready, h_ready, y_ready = sem("silu_gate_ready"), sem("h_ready"), sem("y_ready")
        y_out = [sem(f"y_stored{p}") for p in range(2)]
        gath = [sem(f"results_gathered{t}") for t in range(TT)]
        weighted = sem("first_results_weighted")
        out_done = sem("out_stored")
        xg_scaled = sem("rows_scaled")
        pe_passed, pool_passed = sem("pe_passed_waits"), sem("pool_passed_waits")
        prod_ready = sem("out_ready")

        stream = dense_stream()

        def source(kind, u):
            if kind in ("ada0", "ada1"):
                w = a["ada_w0" if kind == "ada0" else "ada_w1"]
                return w[:, u * W:(u + 1) * W].rearrange("(k p) n -> p k n", p=P)
            if kind == "mod2":
                return a["w_mod_2"][0][:, u * W:(u + 1) * W].rearrange("(k p) n -> p k n", p=P)
            if kind == "win2":
                return a["w_in_2"][0][:, u * W:(u + 1) * W].rearrange("(k p) n -> p k n", p=P)
            if kind == "wout2":
                return a["w_out_2"][0][:, u * W:(u + 1) * W].rearrange("(k p) n -> p k n", p=P)
            if kind == "win1":
                lo = (0, 512, 704, 1216)[u]
                hi = (512, 704, 1216, 1728)[u]
                return a["w_in1"][:, lo:hi].rearrange("(k p) n -> p k n", p=P)
            if kind == "wqb":
                return a["w_q_b"][:, u * 768:(u + 1) * 768].rearrange("(k p) n -> p k n", p=P)
            if kind == "wkvb":
                return a["w_kv_b"].rearrange("(k p) n -> p k n", p=P)
            w = a[{"win0": "w_in0", "wout0": "w_out0", "wout1": "w_out1"}[kind]]
            return w[:, u * W:(u + 1) * W].rearrange("(k p) n -> p k n", p=P)

        def unit_parts(n):
            kind, u = stream[n]
            if kind != "wqb":
                return [(unit_view(n), source(kind, u))]
            w = source(kind, u).rearrange("p k (h c) -> p k h c", h=4)
            nope, pe = wqb_views(n)
            return [(nope[:, k], w[:, k, :, 0:NOPE]) for k in range(3)] + [(pe[:, k], w[:, k, :, NOPE:]) for k in range(3)]

        def wqb_views(n):
            slot = ring[n % RING]
            return (slot[:, 0:3 * 4 * NOPE].rearrange("p (k h c) -> p k h c", k=3, h=4),
                    slot[:, 3 * 4 * NOPE:3 * 4 * (NOPE + ROPE)].rearrange("p (k h c) -> p k h c", k=3, h=4))

        def unit_arrival(n):
            return 16 * sum(len(unit_parts(m)) for m in range(n % RING, n + 1, RING))

        def unit_view(n):
            kt, cols = source(*stream[n]).shape[1:]
            return ring[n % RING][:, 0:kt * cols].rearrange("p (k n) -> p k n", k=kt)

        e_slot = [[ring[0], ring[1], ring[2]], [ring[3], bufA, bufB]]
        e_up = [[e_slot[p][j][:, :].rearrange("p (k n) -> p k n", k=KT) for j in range(2)] for p in range(2)]
        e_down = [e_slot[p][2][:, :].rearrange("p (k n) -> p k n", k=FT) for p in range(2)]
        xg = [bufD[0:SLOTS, p * D:(p + 1) * D] for p in range(2)]
        y_sb = [bufD[0:SLOTS, (2 + p) * D:(3 + p) * D] for p in range(2)]
        xgT = [hT[:, 2 * p:2 * p + 2, :].rearrange("p b n -> p (b n)").rearrange("p (k s) -> p k s", k=KT) for p in range(2)]
        xg_t = hT[:, 4:6, :].rearrange("p b n -> p (b n)").rearrange("p (k s) -> p k s", k=KT)
        BANK_K = W // SLOTS
        hTe = [mix[:, p, 0:FT * SLOTS].rearrange("p (f s) -> p f s", f=FT) for p in range(2)]
        sg = [probsT[:, p, 0:FT * SLOTS] for p in range(2)]
        wg_d = a["w_exp_gate_2"][0]
        wu_d = a["w_exp_up_2"][0]
        wd_d = a["w_exp_down_2"][0]

        block = ctx.enter_context(nc.Block())

        @block.sync
        def _(sp):
            for n in range(len(stream)):
                if n >= RING:
                    sp.wait_ge(unit_used, n - RING + 1)
                for dst, src in unit_parts(n):
                    sp.dma_start(dst, src).then_inc(w_in[n % RING], 16)

            def load_expert(p, e):
                for j, w in enumerate((wg_d, wu_d, wd_d)):
                    src = w[bass.ds(e, 1), :, :].rearrange("o (k p) n -> p (o k) n", p=P)
                    dst = e_up[p][j] if j < 2 else e_down[p]
                    sp.dma_start(dst, src).then_inc(e_in[p][j], 16)

            n_dense = len(stream)
            for p in range(2):
                for j, w in enumerate((wg_d, wu_d, wd_d)):
                    slot = 3 * p + j
                    if slot < RING:
                        last = max(n for n in range(n_dense) if n % RING == slot)
                        sp.wait_ge(unit_used, last + 1)
                    dst = e_up[p][j] if j < 2 else e_down[p]
                    sp.dma_start(dst, w[p].rearrange("(k p) n -> p k n", p=P)).then_inc(e_in[p][j], 16)
            with sp.Fori(1, EXPERTS // 2) as i:
                for p in range(2):
                    for j, w in enumerate((wg_d, wu_d, wd_d)):
                        sp.wait_ge((gate_done, up_done, down_done)[j], 2 * i + p - 1)
                        src = w[bass.ds(2 * i + p, 1), :, :].rearrange("o (k p) n -> p (o k) n", p=P)
                        dst = e_up[p][j] if j < 2 else e_down[p]
                        sp.dma_start(dst, src).then_inc(e_in[p][j], 16)
            sp.wait_ge(over_ready, 1)
            n_over = sp.value_load(over_ids[0:1, OVER:OVER + 1], min_val=0, max_val=OVER)
            with sp.If(n_over > 0), sp.Fori(0, n_over) as k:
                sp.wait_ge(down_done, EXPERTS + k)
                e = sp.value_load(over_ids[0:1, bass.ds(k, 1)], min_val=0, max_val=EXPERTS - 1)
                load_expert(0, e)
            for tt in range(TT):
                sp.wait_ge(prod_ready, tt + 1)
                sp.dma_start(out[0][tt * P:(tt + 1) * P, :], bufA[:, tt * D:(tt + 1) * D]).then_inc(out_done, 16)
            sp.wait_ge(out_done, 16 * TT)

        @block.tensor
        def _(pe):
            act_banks = Banks(psum[0:4], act_filled, act_freed)
            tr_banks = Banks(psum[4:6], tr_filled, tr_freed)
            dve_banks = Banks(psum[6:8], dve_filled, dve_freed)
            unit = [0]
            mm = nc.tensor.matmul

            def open_unit(kind):
                n = unit[0]
                assert stream[n][0] == kind
                pe.wait_ge(w_in[n % RING], unit_arrival(n))
                unit[0] += 1
                return unit_view(n)

            def modulate(kind, count, layer):
                bank = dve_banks.claim(pe)
                for u in range(count):
                    w = open_unit(kind)
                    for j in range(4):
                        for k in range(KT):
                            last = mm(bank[:, 4 * u + j:4 * u + j + 1], w[:, k, j * P:(j + 1) * P],
                                      silu_c[:, 8 * layer + k:8 * layer + k + 1], start=(k == 0), stop=(k == KT - 1))
                    if u < count - 1:
                        last.then_inc(unit_used, 1)
                    else:
                        last.then_inc(dve_filled, 1)
                pe.wait_ge(dve_filled, dve_banks.n)
                pe.sem_inc(unit_used, 1)

            def transposes(banks, filled, pieces):
                bank = banks.claim(pe)
                for i, piece in enumerate(pieces):
                    last = nc.tensor.transpose(bank[:, i * P:(i + 1) * P], piece, ident)
                last.then_inc(filled, 1)

            def norm_transposes(n):
                pe.wait_ge(xn_ready, TT * (n + 1))
                for k in range(KT):
                    pieces = [C_tok[:, t, k * P:(k + 1) * P] for t in range(TT)]
                    if k % 2 == 0:
                        transposes(act_banks, act_filled, pieces)
                    else:
                        transposes(dve_banks, dve_filled, pieces)
                pe.wait_ge(hT_act, 4 * (n + 1))
                pe.wait_ge(hT_dve, 4 * (n + 1))

            def features(w, lo, kts, src, banks, filled):
                bank = banks.claim(pe)
                for k in range(kts):
                    last = mm(bank[:, :], w[:, k, lo:lo + P], src[:, k, :],
                              start=(k == 0), stop=(k == kts - 1))
                last.then_inc(filled, 1)

            def tokens(rhs, cols, kts, src, t, banks, filled):
                bank = banks.claim(pe)
                for k in range(kts):
                    last = mm(bank[:, 0:cols], src[:, k, t * P:(t + 1) * P], rhs(k), start=(k == 0), stop=(k == kts - 1))
                last.then_inc(filled, 1)

            def close_unit(filled, banks):
                pe.wait_ge(filled, banks.n)
                pe.sem_inc(unit_used, 1)

            rope_jobs = [0]

            def rotate(src):
                rope_jobs[0] += 1
                bank = dve_banks.claim(pe)
                mm(bank[:, :], rot, src, start=True, stop=True).then_inc(dve_filled, 1)

            def gate_broadcast(n):
                pe.wait_ge(gatecols_ready, n + 1)
                for half in range(2):
                    bank = act_banks.claim(pe)
                    for j in range(4):
                        last = mm(bank[:, j * P:(j + 1) * P], gate_cols[:, 4 * half + j, :], ident, start=True, stop=True)
                    last.then_inc(act_filled, 1)

            def project_out(kind, src):
                for u in range(2):
                    w = open_unit(kind)
                    for t in range(TT):
                        tokens(lambda k: w[:, k, :], W, KT, src, t, dve_banks, dve_filled)
                    close_unit(dve_filled, dve_banks)

            def attention(base, score, width, weights, ready, pv, splits):
                n_steps = TT * HEADS
                tr_base = tr_banks.n

                def scores(i):
                    for c in range(splits):
                        bank = act_banks.claim(pe)
                        score(bank, i // HEADS, i % HEADS, c).then_inc(act_filled, 1)

                def flip(i):
                    pe.wait_ge(ready, base[1] + i + 1)
                    transposes(tr_banks, tr_filled, [weights(i)[:, j * P:(j + 1) * P] for j in range(width(i // HEADS) // P)])

                def output(i):
                    pe.wait_ge(tr_freed, tr_base + i + 1)
                    bank = dve_banks.claim(pe)
                    pv(bank, i // HEADS, i % HEADS, probsT[:, i % 2, :]).then_inc(dve_filled, 1)

                scores(0)
                scores(1)
                for i in range(n_steps):
                    if i + 2 < n_steps:
                        scores(i + 2)
                    flip(i)
                    if i >= 1:
                        output(i - 1)
                output(n_steps - 1)

            pe.wait_ge(s_in, N_IN * 16)
            for rows, n in ((bufD[:, 0:P], R1_ROWS), (bufD[:, P:2 * P], R2_ROWS), (bufD[:, 2 * P:3 * P], R3_ROWS)):
                bank = act_banks.claim(pe)
                nc.tensor.transpose(bank[:, 0:n], rows[0:n, :], ident[0:n, 0:n]).then_inc(act_filled, 1)
            pe.wait_ge(silu_ready, 1)

            modulate("ada0", 4, 0)
            norm_transposes(0)
            for u in range(4):
                w = open_unit("win0")
                for j in range(4):
                    features(w, j * P, KT, hT, act_banks, act_filled)
                    f = 4 * u + j
                    if f >= 1:
                        pe.wait_ge(raw_ready, f)
                        rotate(probs[:, (f - 1) % 3, :])
                close_unit(act_filled, act_banks)
            for u in range(4):
                w = open_unit("win0")
                for t in range(TT):
                    if u < 2:
                        tokens(lambda k: w[:, k, :], W, KT, hT, t, dve_banks, dve_filled)
                    else:
                        tokens(lambda k: w[:, k, :], W, KT, hT, t, act_banks, act_filled)
                    if u == 0 and t == 0:
                        pe.wait_ge(raw_ready, 16)
                        rotate(probs[:, 15 % 3, :])
                close_unit(*((dve_filled, dve_banks) if u < 2 else (act_filled, act_banks)))
            pe.wait_ge(rope_ready, 16)
            pe.wait_ge(v_ready, 8)

            def score0(bank, t, h, c):
                r = slice(DA_DIM * c, DA_DIM * (c + 1))
                return mm(bank[:, :], A8[r, h, t * P:(t + 1) * P], B8[r, h, :], start=True, stop=True)

            def pv_heads(bank, t, h, pT):
                for j in range(TT):
                    last = mm(bank[:, 0:P], pT[:, j * P:(j + 1) * P], C_tok[:, j, h * P:(h + 1) * P],
                              start=(j == 0), stop=(j == TT - 1))
                return last

            attention((0, 0), score0, lambda t: T, lambda i: mix[:, i % 3, :], mix_ready, pv_heads, 2)
            modulate("ada0", 2, 0)
            gate_broadcast(0)
            pe.wait_ge(og_ready, TT)
            for k in range(KT):
                transposes(tr_banks, tr_filled, [D_tok[:, t, k * P:(k + 1) * P] for t in range(TT)])
            pe.wait_ge(oT_ready, 8)
            project_out("wout0", A8)

            modulate("ada1", 4, 0)
            norm_transposes(1)
            for u, cols in enumerate((512, 192, 512, 512)):
                w = open_unit("win1")
                for t in range(TT):
                    tokens(lambda k: w[:, k, :], cols, KT, hT, t, act_banks, act_filled)
                close_unit(act_filled, act_banks)
            pe.wait_ge(n1_ready, TT)
            latents = tok(bufA, 768)
            for b in range(6):
                transposes(tr_banks, tr_filled, [latents[:, t, b * P:(b + 1) * P] for t in range(TT)])
            pe.wait_ge(nT_ready, 6)
            rotate(B8[:, 5, :])
            q_pairs = 0
            for u in range(2):
                open_unit("wqb")
                nope, rotary = wqb_views(unit[0] - 1)
                for j in range(4):
                    features(nope[:, :, j, :], 0, 3, B8, act_banks, act_filled)
                for j in range(2):
                    pair = rotary[:, :, 2 * j:2 * j + 2, :].rearrange("p k h c -> p k (h c)")
                    features(pair, 0, 3, B8, act_banks, act_filled)
                    q_pairs += 1
                    if q_pairs >= 2:
                        pe.wait_ge(raw_ready, 16 + q_pairs - 1)
                        rotate(probs[:, (q_pairs - 2) % 3, :])
                close_unit(act_filled, act_banks)
            w = open_unit("wkvb")
            for h in range(HEADS):
                features(w, h * 256, 2, B8[:, 3:5, :], act_banks, act_filled)
                if h == 0:
                    pe.wait_ge(raw_ready, 16 + 4)
                    rotate(probs[:, 0, :])
            for nb in range(2):
                wv = w[:, :, nb * 1024:(nb + 1) * 1024].rearrange("p k (h c) -> p k h c", h=4)[:, :, :, NOPE:]
                for t in range(TT):
                    tokens(lambda k: wv[:, k, :, :], W, 2, B8[:, 3:5, :], t, dve_banks, dve_filled)
            close_unit(dve_filled, dve_banks)
            pe.wait_ge(rope_ready, 21)
            pe.wait_ge(qk_ready, 16)
            pe.wait_ge(v_ready, 16)
            E5 = feat(bufE, 5)

            def score1(bank, t, h, c):
                mm(bank[:, :], hT[:, h, t * P:(t + 1) * P], A8[:, h, :], start=True, stop=False)
                r = slice(ROPE * (h % 2), ROPE * (h % 2) + ROPE)
                return mm(bank[:, :], E5[r, h // 2, t * P:(t + 1) * P], E5[r, 4, :], start=False, stop=True)

            attention((32, 32), score1, lambda t: T, lambda i: probs[:, i % 2, :], exp_ready, pv_heads, 1)
            modulate("ada1", 2, 0)
            gate_broadcast(1)
            pe.wait_ge(og_ready, 2 * TT)
            for k in range(KT):
                transposes(tr_banks, tr_filled, [D_tok[:, t, k * P:(k + 1) * P] for t in range(TT)])
            pe.wait_ge(oT_ready, 16)
            project_out("wout1", A8)

            modulate("mod2", 4, 1)
            norm_transposes(2)
            wa = open_unit("win2")
            wb = open_unit("win2")
            for j in range(CH):
                features(wb, j * P, KT, hT, act_banks, act_filled)
                features(wa, j * P, KT, hT, dve_banks, dve_filled)
            close_unit(dve_filled, dve_banks)
            close_unit(dve_filled, dve_banks)
            for u in range(3):
                w = open_unit("win2")
                for j in range(4):
                    if u < 2:
                        features(w, j * P, KT, hT, act_banks, act_filled)
                    else:
                        tokens(lambda k: w[:, k, :], W, KT, hT, j, act_banks, act_filled)
                close_unit(act_filled, act_banks)
            pe.wait_ge(conv_ready, CH)
            conv = feat(bufD, CH, 2048)
            for t in range(TT):
                transposes(dve_banks, dve_filled, [conv[:, j, t * P:(t + 1) * P] for j in range(CH)])
            pe.wait_ge(ln_ready, TT)
            lnorm = tok(bufC, W)
            for j in range(CH):
                transposes(tr_banks, tr_filled, [lnorm[:, t, j * P:(j + 1) * P] for t in range(TT)])
            pe.wait_ge(qk_ready, 16 + 12)
            v2 = tok(bufE, W)

            def score2(bank, t, h, c):
                r = slice(ALIBI_DIM * (h % 2), ALIBI_DIM * (h % 2 + 1))
                n = P * (t + 1)
                return mm(bank[:, 0:n], A8[r, h // 2, t * P:(t + 1) * P], A8[r, 4 + h // 2, 0:n], start=True, stop=True)

            def pv2(bank, t, h, pT):
                for j in range(t + 1):
                    last = mm(bank[:, 0:ALIBI_DIM], pT[:, j * P:(j + 1) * P], v2[:, j, h * ALIBI_DIM:(h + 1) * ALIBI_DIM],
                              start=(j == 0), stop=(j == t))
                return last

            attention((64, 64), score2, lambda t: P * (t + 1), lambda i: probs[:, i % 2, :], exp_ready, pv2, 1)
            modulate("mod2", 2, 1)
            gate_broadcast(2)
            pe.wait_ge(og_ready, 3 * TT)
            attn2 = tok(bufD, W)
            for k in range(4):
                transposes(tr_banks, tr_filled, [attn2[:, t, k * P:(k + 1) * P] for t in range(TT)])
            pe.wait_ge(oT_ready, 16 + 8)
            project_out("wout2", hT)

            modulate("mod2", 4, 1)
            norm_transposes(3)
            bank = dve_banks.claim(pe)
            R = GROUPS + EXPERTS
            for t in range(TT):
                for k in range(KT):
                    last = mm(bank[:, t * R:(t + 1) * R], hT[:, k, t * P:(t + 1) * P], w_router[:, k, :],
                              start=(k == 0), stop=(k == KT - 1))
            last.then_inc(dve_filled, 1)
            pe.wait_ge(mask_ready, 1)
            bank = dve_banks.claim(pe)
            for t in range(TT + 1):
                o = bank[:, t * EXPERTS:(t + 1) * EXPERTS]
                for j in range(t):
                    last = mm(o, ones, mask_v[:, j, :], start=(j == 0), stop=(t == TT and j == t - 1))
                if t < TT:
                    last = mm(o, upper, mask_v[:, t, :], start=(t == 0), stop=True)
            last.then_inc(dve_filled, 1)
            modulate("mod2", 2, 1)
            gate_broadcast(3)
            pe.wait_ge(act_freed, act_banks.n)
            pe.wait_ge(tr_freed, tr_banks.n)
            pe.wait_ge(dve_freed, dve_banks.n)

            def flip_rows(p, loads, n, first=False):
                pe.wait_ge(xg_in[p], loads)
                if not first:
                    pe.wait_ge(xgT_ready, n)
                pe.sem_inc(pe_passed, 1)
                for k in range(KT):
                    col = k % BANK_K * SLOTS
                    last = nc.tensor.transpose(psum[k // BANK_K][:, col:col + SLOTS], xg[p][:, k * P:(k + 1) * P],
                                               ident[0:SLOTS, 0:SLOTS])
                last.then_inc(xg_read, 1)

            def item(p, loads, n, first=False, ahead=None):
                for j, (role, done) in enumerate(((2, gate_done), (3, up_done))):
                    pe.wait_ge(e_in[p][j], loads)
                    if j == 0:
                        pe.wait_ge(xgT_ready, n + 1)
                        if not first:
                            pe.wait_ge(sg_ready, n)
                    elif not first:
                        pe.wait_ge(h_ready, n)
                    for f in range(FT):
                        for k in range(KT):
                            last = mm(psum[role][:, f * SLOTS:(f + 1) * SLOTS], e_up[p][j][:, k, f * P:(f + 1) * P],
                                      xgT[p][:, k, :], start=(k == 0), stop=(k == KT - 1))
                    last.then_inc(done, 1)
                if ahead is not None:
                    ahead()
                pe.wait_ge(e_in[p][2], loads)
                pe.wait_ge(h_ready, n + 1)
                if not first:
                    pe.wait_ge(y_ready, n)
                for half in range(2):
                    for f in range(FT):
                        last = mm(psum[4 + 2 * p + half][0:SLOTS, :], hTe[p][:, f, :],
                                  e_down[p][:, f, half * W:(half + 1) * W], start=(f == 0), stop=(f == FT - 1))
                last.then_inc(down_done, 1)

            flip_rows(0, 16, 0, first=True)
            item(0, 16, 0, first=True, ahead=lambda: flip_rows(1, 16, 1))
            item(1, 16, 1, ahead=lambda: flip_rows(0, 32, 2))
            with pe.Fori(1, EXPERTS // 2 - 1) as i:
                item(0, 16 * i + 16, 2 * i, ahead=lambda: flip_rows(1, 16 * i + 16, 2 * i + 1))
                item(1, 16 * i + 16, 2 * i + 1, ahead=lambda: flip_rows(0, 16 * i + 32, 2 * i + 2))
            half_n = EXPERTS // 2
            item(0, 16 * half_n, EXPERTS - 2, ahead=lambda: flip_rows(1, 16 * half_n, EXPERTS - 1))
            item(1, 16 * half_n, EXPERTS - 1)
            pe.wait_ge(over_ready, 1)
            n_over = pe.value_load(over_ids[0:1, OVER:OVER + 1], min_val=0, max_val=OVER)
            with pe.If(n_over > 0), pe.Fori(0, n_over) as k:
                flip_rows(0, 16 * half_n + 16 + 16 * k, EXPERTS + k)
                item(0, 16 * half_n + 16 + 16 * k, EXPERTS + k)

        @block.scalar
        def _(act):
            steps = Steps(act, act_step)
            act_banks = Banks(psum[0:4], act_filled, act_freed)
            tr_banks = Banks(psum[4:6], tr_filled, tr_freed)
            fn = nc.scalar.activation

            for dst, src in in_loads:
                act.dma_start(dst, src).then_inc(s_in, 16)
            act.dma_start(x[:, :, :], a["x"][0].rearrange("(t p) d -> p t d", p=P)).then_inc(s_xin, 16)
            act.dma_start(norm_row[:, :], a["final_norm_g"].unsqueeze(0).to_broadcast([P, D])).then_inc(norm_row_in, 16)

            def evac(banks, freed, dst, cols, func=ACT.Copy, **kw):
                bank = banks.take(act)
                return fn(dst, bank[:, 0:cols], func, **kw)

            def squares(n, need_x):
                if need_x is None:
                    act.wait_ge(s_xin, 16)
                else:
                    act.wait_ge(x_ready, need_x)
                for t in range(TT):
                    fn(C_tok[:, t, :], x[:, t, :], ACT.Square, accum_out=ss[:, t:t + 1]).then_inc(squares_ready, 1)

            def norm_evac(n, shift):
                act.wait_ge(aff_ready, n + 1)
                for k in range(0, KT, 2):
                    bank = act_banks.take(act)
                    fn(hT[:, k, :], bank[:, :], ACT.Identity, bias=mods[:, k:k + 1],
                       scale=aff[:, k:k + 1]).then_inc(act_freed, 1)
                act.wait_ge(act_freed, act_banks.n)
                act.sem_inc(hT_act, 4)

            def gate_evac(n):
                for half in range(2):
                    bank = act_banks.take(act)
                    fn(gate_row[:, half * W:(half + 1) * W], bank[:, :], ACT.Copy).then_inc(act_freed, 1)
                act.wait_ge(act_freed, act_banks.n)
                act.sem_inc(gate_ready, 1)

            def attention(base, width, splits, scale, stage):
                n_steps = TT * HEADS

                def exps(i):
                    act.wait_ge(max_ready, base + i + 1)
                    for c in range(splits):
                        bank = act_banks.take(act)
                        w = width(i // HEADS)
                        j = splits * i + c
                        ins = fn(probs[:, stage(i, c), 0:w], bank[:, 0:w], ACT.Exp, bias=negmax[:, j:j + 1],
                                 scale=scale, accum_out=sums[:, j:j + 1])
                        ins.then_inc(act_freed, 1)
                    act.wait_ge(act_freed, act_banks.n)
                    act.sem_inc(exp_ready, 1)

                def copy_T(i):
                    bank = tr_banks.take(act)
                    w = width(i // HEADS)
                    fn(probsT[:, i % 2, 0:w], bank[:, 0:w], ACT.Copy).then_inc(tr_freed, 1)

                exps(0)
                for i in range(n_steps):
                    if i + 1 < n_steps:
                        exps(i + 1)
                    copy_T(i)

            def outputs_T(dst, scales, n):
                for k in range(n):
                    bank = tr_banks.take(act)
                    fn(dst[:, k, :], bank[:, :], ACT.Copy, scale=scales(k)).then_inc(tr_freed, 1)
                act.wait_ge(tr_freed, tr_banks.n)
                act.sem_inc(oT_ready, n)

            for dst, n in ((col1, R1_ROWS), (col2, R2_ROWS), (col3, R3_ROWS)):
                bank = act_banks.take(act)
                fn(dst[:, :], bank[:, 0:n], ACT.Copy).then_inc(act_freed, 1)
            act.wait_ge(act_freed, 3)
            fn(silu_c[:, :], col2[:, R2["c"]:R2["c"] + 16], ACT.Silu).then_inc(silu_ready, 1)
            squares(0, None)
            act.wait_ge(angles_ready, 1)
            steps(fn(cosT[:, :], cosT[:, :], ACT.Sin))
            fn(sinT[:, :], sinT[:, :], ACT.Sin).then_inc(sincos_ready, 1)
            act.wait_ge(lam_dots, 1)
            fn(lam[:, 0:2], tiny[:, 0:2], ACT.Exp).then_inc(lam_exps, 1)

            norm_evac(0, 0)
            for f in range(16):
                bank = act_banks.take(act)
                if f >= 3:
                    act.wait_ge(rope_ready, f - 2)
                fn(probs[:, f % 3, :], bank[:, :], ACT.Copy, scale=0.125 if f < 8 else 1.0).then_inc(act_freed, 1)
                act.wait_ge(act_freed, act_banks.n)
                act.sem_inc(raw_ready, 1)
            for u in range(2):
                for t in range(TT):
                    bank = act_banks.take(act)
                    fn(D_tok[:, t, u * W:(u + 1) * W], bank[:, :], ACT.Silu).then_inc(act_freed, 1)
            act.wait_ge(act_freed, act_banks.n)
            act.sem_inc(z_ready, 1)
            act.wait_ge(zero_ready, 1)
            xs_flat = xs.rearrange("(p m) d -> p (m d)", p=P).rearrange("p (a b) -> p a b", b=P)
            act.dma_start(xs_flat, zero[:, :].unsqueeze(1).to_broadcast([P, xs_flat.shape[1], P])).then_inc(zeros_out, 16)
            ys_flat = ys[EXPERTS * SLOTS:, :].rearrange("(p m) d -> p (m d)", p=P).rearrange("p (a b) -> p a b", b=P)
            act.dma_start(ys_flat, zero[:, :].unsqueeze(1).to_broadcast([P, ys_flat.shape[1], P])).then_inc(zeros_out, 16)
            attention(0, lambda t: T, 2, 1.0, lambda i, c: 2 * (i % 2) + c)
            gate_evac(0)
            steps(fn(tiny[:, 4:5], col2[:, R2["subln_g"]:R2["subln_g"] + 1], ACT.Copy, scale=1.0 - LAMBDA_INIT))
            steps.settle()
            outputs_T(A8, lambda k: tiny[:, 4:5], 8)

            squares(1, 1)
            norm_evac(1, 0)
            latents = tok(bufA, 768)
            for u, (lo, cols) in enumerate(((0, 512), (512, 192))):
                for t in range(TT):
                    bank = act_banks.take(act)
                    fn(latents[:, t, lo:lo + cols], bank[:, 0:cols], ACT.Copy).then_inc(act_freed, 1)
            act.wait_ge(act_freed, act_banks.n)
            act.sem_inc(raw1_ready, 1)
            for u in range(2):
                for t in range(TT):
                    bank = act_banks.take(act)
                    fn(D_tok[:, t, u * W:(u + 1) * W], bank[:, :], ACT.Silu).then_inc(act_freed, 1)
            act.wait_ge(act_freed, act_banks.n)
            act.sem_inc(z_ready, 1)
            for b in range(6):
                bank = tr_banks.take(act)
                kw = {} if b == 5 else {"scale": col2[:, R2["qa_g"] + b:R2["qa_g"] + b + 1]}
                fn(B8[:, b, :], bank[:, :], ACT.Copy, **kw).then_inc(tr_freed, 1)
            act.wait_ge(tr_freed, tr_banks.n)
            act.sem_inc(nT_ready, 6)
            pair = 0
            for u in range(2):
                for j in range(6):
                    bank = act_banks.take(act)
                    if j < 4:
                        fn(hT[:, 4 * u + j, :], bank[:, :], ACT.Copy).then_inc(act_freed, 1)
                        continue
                    if pair == 3:
                        act.wait_ge(rope_ready, 16 + 2)
                    fn(probs[:, pair % 3, :], bank[:, :], ACT.Copy).then_inc(act_freed, 1)
                    act.wait_ge(act_freed, act_banks.n)
                    act.sem_inc(raw_ready, 1)
                    pair += 1
            for h in range(HEADS):
                bank = act_banks.take(act)
                fn(A8[:, h, :], bank[:, :], ACT.Copy).then_inc(act_freed, 1)
            act.wait_ge(act_freed, act_banks.n)
            act.sem_inc(qk_ready, 16)
            attention(32, lambda t: T, 1, MLA_SCALE, lambda i, c: i % 2)
            gate_evac(1)
            outputs_T(A8, lambda k: 1.0, 8)
            squares(2, 2)

            act.dma_start(bufB[:, :], a["alibi"]).then_inc(alibi_in, 16)
            squares(3, 3)
            act.wait_ge(norm_row_used, 1)
            act.dma_start(norm_row[:, :], a["g_final_2"].unsqueeze(0).to_broadcast([P, D])).then_inc(norm_row_in, 16)
            norm_evac(2, 0)
            for j in range(CH):
                bank = act_banks.take(act)
                if j >= 2:
                    act.wait_ge(u_used, j - 1)
                fn(mix[:, j % 2, :], bank[:, :], ACT.Sigmoid).then_inc(act_freed, 1)
                act.wait_ge(act_freed, act_banks.n)
                act.sem_inc(sig_ready, 1)
            v2 = tok(bufE, W)
            for u in range(3):
                for j in range(4):
                    bank = act_banks.take(act)
                    dst = A8[:, 4 * u + j, :] if u < 2 else v2[:, j, :]
                    fn(dst, bank[:, :], ACT.Copy, scale=0.125 if u == 0 else 1.0).then_inc(act_freed, 1)
            act.wait_ge(act_freed, act_banks.n)
            act.sem_inc(qk_ready, 12)
            for j in range(CH):
                bank = tr_banks.take(act)
                fn(hT[:, 4 + j, :], bank[:, :], ACT.Silu, bias=col2[:, R2["ln_b"] + j:R2["ln_b"] + j + 1],
                   scale=col2[:, R2["ln_g"] + j:R2["ln_g"] + j + 1]).then_inc(tr_freed, 1)
            act.wait_ge(tr_freed, tr_banks.n)
            act.sem_inc(oT_ready, CH)
            attention(64, lambda t: P * (t + 1), 1, 1.0, lambda i, c: i % 2)
            gate_evac(2)
            outputs_T(hT, lambda k: 1.0, 4)
            squares(4, 4)
            norm_evac(3, 0)
            act.wait_ge(gexp_in, 1)
            fn(rt_gexp, rt_gexp, ACT.Exp).then_inc(gexp_out, 1)
            act.wait_ge(gexp_in, 2)
            fn(rt_d, rt_d, ACT.Exp).then_inc(gexp_out, 1)
            gate_evac(3)

            def item(p, n, stores, first=False):
                act.wait_ge(gate_done, n + 1)
                if not first:
                    act.wait_ge(h_ready, n - 1)
                fn(sg[p], psum[2][:, 0:FT * SLOTS], ACT.Silu).then_inc(sg_ready, 1)
                act.wait_ge(down_done, n + 1)
                if not first:
                    act.wait_ge(y_out[p], stores)
                steps(fn(y_sb[p][:, 0:W], psum[4 + 2 * p][0:SLOTS, :], ACT.Copy))
                fn(y_sb[p][:, W:D], psum[5 + 2 * p][0:SLOTS, :], ACT.Copy).then_inc(y_ready, 1)
                act.wait_ge(y_ready, n + 1)
                act.dma_start(ys[bass.ds(n * SLOTS, SLOTS), :], y_sb[p]).then_inc(y_out[p], 16)

            item(0, 0, 0, first=True)
            item(1, 1, 0, first=True)
            with act.Fori(1, EXPERTS // 2) as i:
                item(0, 2 * i, 16 * i)
                item(1, 2 * i + 1, 16 * i)
            act.wait_ge(over_ready, 1)
            act.wait_ge(zeros_out, 32)
            n_over = act.value_load(over_ids[0:1, OVER:OVER + 1], min_val=0, max_val=OVER)
            with act.If(n_over > 0), act.Fori(0, n_over) as k:
                item(0, EXPERTS + k, 8 * EXPERTS + 16 * k)
            def weigh(t):
                act.wait_ge(gath[t], 32)
                y0 = ring[0][:, t * D:(t + 1) * D]
                fn(y0, y0, ACT.Copy, scale=wts[:, 0, t:t + 1]).then_inc(weighted, 1)

            weigh(0)
            for t in range(TT):
                if t < TT - 1:
                    weigh(t + 1)
                act.wait_ge(x_ready, 5 + t)
                fn(bufC[:, t * D:(t + 1) * D], x[:, t, :], ACT.Square, accum_out=ss[:, t:t + 1]).then_inc(squares_ready, 1)

        @block.gpsimd
        def _(pool):
            steps = Steps(pool, pool_step)
            gp = nc.gpsimd

            steps(gp.memset(half_neg[:, :], -0.5))
            gp.memset(zero[:, :], 0.0).then_inc(zero_ready, 1)

            def rstd(cols, width):
                s, p0, p1, p2 = ss[:, 0:cols], pw[:, 0, 0:cols], pw[:, 1, 0:cols], pw[:, 2, 0:cols]
                steps(gp.tensor_scalar(p0, s, 1.0 / width, EPS, ALU.mult, ALU.add))
                steps.settle()
                steps(gp.tensor_tensor(p1, p0, half_neg[:, 0:cols], ALU.pow))
                steps.settle()
                steps(gp.tensor_tensor(p2, p1, p1, ALU.mult))
                steps.settle()
                steps(gp.tensor_tensor(p2, p2, p0, ALU.mult))
                steps.settle()
                steps(gp.tensor_scalar(p2, p2, -0.5, 1.5, ALU.mult, ALU.add))
                steps.settle()
                gp.tensor_tensor(s, p1, p2, ALU.mult).then_inc(rstd_ready, 1)

            count = 0

            def norm_rstd(width=D, cols=TT, arrivals=TT):
                nonlocal count
                count += arrivals
                pool.wait_ge(squares_ready, count)
                rstd(cols, width)

            norm_rstd()
            for t in range(TT):
                norm_rstd(128, 8, 1)
            norm_rstd()
            norm_rstd(1, 8, 1)
            norm_rstd()
            norm_rstd()
            norm_rstd(W, 4, 1)
            norm_rstd()
            pool.wait_ge(dest_ready, 1)
            pool.wait_ge(zeros_out, 32)
            for t in range(TT):
                for k in range(2):
                    gp.indirect_dma_start(xs[:, :], bass.IndirectOffsetOnAxis(ap=dest[:, k, t:t + 1], axis=0),
                                          C_tok[:, t, :], None).then_inc(rows_out, 16)
            pool.wait_ge(rows_out, 16 * 2 * TT)

            def load_rows(p, n):
                gp.dma_start(xg[p], xs[bass.ds(n * SLOTS, SLOTS), :]).then_inc(xg_in[p], 16)

            load_rows(0, 0)
            load_rows(1, 1)
            with pool.Fori(1, EXPERTS // 2) as i:
                for p in range(2):
                    pool.wait_ge(xg_read, 2 * i + p - 1)
                    load_rows(p, 2 * i + p)
            pool.wait_ge(over_ready, 1)
            n_over = pool.value_load(over_ids[0:1, OVER:OVER + 1], min_val=0, max_val=OVER)
            with pool.If(n_over > 0), pool.Fori(0, n_over) as k:
                pool.wait_ge(xg_read, EXPERTS + k)
                load_rows(0, EXPERTS + k)
            pool.wait_ge(y_out[0], 8 * EXPERTS + 16 * n_over)
            pool.wait_ge(y_out[1], 8 * EXPERTS)
            pool.sem_inc(pool_passed, 1)
            for t in range(TT):
                for k in range(2):
                    gp.indirect_dma_start(ring[k][:, t * D:(t + 1) * D], None, ys[:, :],
                                          bass.IndirectOffsetOnAxis(ap=dest[:, k, t:t + 1], axis=0)).then_inc(gath[t], 16)
            norm_rstd()

        @block.vector
        def _(dve):
            steps = Steps(dve, dve_step)
            dve_banks = Banks(psum[6:8], dve_filled, dve_freed)
            act_banks = Banks(psum[0:4], act_filled, act_freed)
            v = nc.vector

            def chain(ins):
                steps(ins)
                steps.settle()

            rstds = [0]

            def wait_rstd():
                rstds[0] += 1
                dve.wait_ge(rstd_ready, rstds[0])

            def first_of(values, best, n, iota, hits, cands, hot, idx):
                bb = lambda c: c.unsqueeze(2).to_broadcast([P, TT, n])
                ib = iota.unsqueeze(1).to_broadcast([P, TT, n])
                chain(v.tensor_tensor(hits, values, bb(best), ALU.is_ge))
                chain(v.scalar_tensor_tensor(out=cands, in0=hits, scalar=-100.0, in1=ib, op0=ALU.mult, op1=ALU.add))
                chain(v.tensor_reduce(idx, cands, AX.X, ALU.min))
                chain(v.tensor_scalar(idx, idx, 100.0, None, ALU.add))
                chain(v.tensor_tensor(hot, ib, bb(idx), ALU.is_equal))

            def route():
                iota4 = k_sb[:, K_IOTA4:K_IOTA4 + GROUPS]
                iota32 = k_sb[:, K_IOTA32:K_IOTA32 + NE]
                items = k_sb[:, K_ITEM:K_ITEM + OVER]
                g_idx, g_max, m1, m2, pg, w1, r, ob, j, slot = by_t[3:13]
                bank = dve_banks.take(dve)
                n = GROUPS + NE
                v.tensor_tensor(logits, bank[:, 0:TT * n].rearrange("p (t n) -> p t n", t=TT),
                                b_router[:, :].unsqueeze(1).to_broadcast([P, TT, n]), ALU.add).then_inc(dve_freed, 1)
                dve.wait_ge(dve_freed, dve_banks.n)
                g_log, e_log = logits[:, :, 0:GROUPS], logits[:, :, GROUPS:]
                chain(v.tensor_reduce(g_max, g_log, AX.X, ALU.max))
                v.tensor_tensor(rt_gexp, g_log, g_max.unsqueeze(2).to_broadcast([P, TT, GROUPS]), ALU.subtract)\
                    .then_inc(gexp_in, 1)
                first_of(g_log, g_max, GROUPS, iota4, g_hit, item_cmp[:, 0, 0:16].rearrange("p (t n) -> p t n", t=TT), g_hot, g_idx)
                chain(v.tensor_scalar(g_hit, g_hot, -NEG, NEG, ALU.mult, ALU.add))
                for t in range(TT):
                    chain(v.tensor_tensor(masked[:, t, :].rearrange("p (g e) -> p g e", g=GROUPS),
                                          e_log[:, t, :].rearrange("p (g e) -> p g e", g=GROUPS),
                                          g_hit[:, t, :].unsqueeze(2).to_broadcast([P, GROUPS, PER_GROUP]), ALU.add))
                chain(v.tensor_reduce(m1, masked, AX.X, ALU.max))
                first_of(masked, m1, NE, iota32, hit, cand, first_hot, first_idx)
                chain(v.scalar_tensor_tensor(out=masked, in0=first_hot, scalar=NEG, in1=masked, op0=ALU.mult, op1=ALU.add))
                chain(v.tensor_reduce(m2, masked, AX.X, ALU.max))
                first_of(masked, m2, NE, iota32, hit, cand, second_hot, second_idx)
                chain(v.tensor_tensor(mask_v, first_hot, second_hot, ALU.add))
                dve.sem_inc(mask_ready, 1)
                v.tensor_tensor(rt_d, m2, m1, ALU.subtract).then_inc(gexp_in, 1)
                bank = dve_banks.take(dve)
                v.tensor_copy(rank_v, bank[:, 0:(TT + 1) * NE].rearrange("p (t n) -> p t n", t=TT + 1)).then_inc(dve_freed, 1)
                dve.wait_ge(dve_freed, dve_banks.n)
                count_e = rank_v[:, TT, :]
                chain(v.tensor_scalar(more, count_e, float(SLOTS), None, ALU.is_gt))
                for m in range(2, MORE + 1):
                    chain(v.scalar_tensor_tensor(out=more, in0=count_e, scalar=float(m * SLOTS), in1=more,
                                                 op0=ALU.is_gt, op1=ALU.add))
                src, dst = more_incl, more_tmp
                chain(v.tensor_copy(src, more))
                for s in (1, 2, 4, 8, 16):
                    chain(v.tensor_copy(dst[:, 0:s], src[:, 0:s]))
                    chain(v.tensor_tensor(dst[:, s:NE], src[:, s:NE], src[:, 0:NE - s], ALU.add))
                    src, dst = dst, src
                incl = src
                chain(v.tensor_tensor(more_before, incl, more, ALU.subtract))
                for k, (hot, idx) in enumerate(((first_hot, first_idx), (second_hot, second_idx))):
                    chain(v.tensor_tensor(cand, hot, rank_v[:, 0:TT, :], ALU.mult))
                    chain(v.tensor_reduce(r, cand, AX.X, ALU.add))
                    chain(v.tensor_tensor(cand, hot, more_before.unsqueeze(1).to_broadcast([P, TT, NE]), ALU.mult))
                    chain(v.tensor_reduce(ob, cand, AX.X, ALU.add))
                    chain(v.tensor_scalar(j, r, float(SLOTS), None, ALU.is_ge))
                    for m in range(2, MORE + 1):
                        chain(v.scalar_tensor_tensor(out=j, in0=r, scalar=float(m * SLOTS), in1=j, op0=ALU.is_ge, op1=ALU.add))
                    chain(v.scalar_tensor_tensor(out=slot, in0=j, scalar=-float(SLOTS), in1=r, op0=ALU.mult, op1=ALU.add))
                    chain(v.scalar_tensor_tensor(out=ob, in0=j, scalar=float(NE - 1), in1=ob, op0=ALU.add, op1=ALU.add))
                    chain(v.tensor_tensor(ob, ob, idx, ALU.subtract))
                    chain(v.tensor_scalar(j, j, 0.0, None, ALU.is_gt))
                    chain(v.tensor_tensor(ob, ob, j, ALU.mult))
                    chain(v.tensor_tensor(ob, ob, idx, ALU.add))
                    chain(v.scalar_tensor_tensor(out=slot, in0=ob, scalar=float(SLOTS), in1=slot, op0=ALU.mult, op1=ALU.add))
                    chain(v.tensor_copy(dest[:, k, :], slot))
                dve.sem_inc(dest_ready, 1)
                chain(v.tensor_tensor(item_cmp, incl.unsqueeze(1).to_broadcast([P, OVER, NE]),
                                      items.unsqueeze(2).to_broadcast([P, OVER, NE]), ALU.is_le))
                chain(v.tensor_reduce(over_f[:, 0:OVER], item_cmp, AX.X, ALU.add))
                chain(v.tensor_scalar(over_f[:, 0:OVER], over_f[:, 0:OVER], float(NE - 1), None, ALU.min))
                chain(v.tensor_copy(over_f[:, OVER:OVER + 1], incl[:, NE - 1:NE]))
                chain(v.tensor_copy(over_ids[:, :], over_f))
                dve.sem_inc(over_ready, 1)
                dve.wait_ge(gexp_out, 2)
                chain(v.tensor_reduce(pg, rt_gexp, AX.X, ALU.add))
                chain(v.reciprocal(pg, pg))
                chain(v.tensor_scalar(w1, rt_d, 1.0, None, ALU.add))
                chain(v.reciprocal(w1, w1))
                chain(v.tensor_tensor(wts[:, 0, :], w1, pg, ALU.mult))
                chain(v.tensor_tensor(wts[:, 1, :], wts[:, 0, :], rt_d, ALU.mult))

            dve.wait_ge(s_in, N_IN * 16)
            pos = bufE[:, 0:T].bitcast(I32)
            ang, turns, r, rabs = (bufE[:, T * n:T * (n + 1)] for n in (1, 2, 3, 4))
            chain(v.tensor_copy(ang, pos))
            chain(v.tensor_scalar(ang, ang, k_sb[:, K_INV:K_INV + 1], None, ALU.mult))
            chain(v.tensor_scalar(turns, ang, 1.0 / TWO_PI, None, ALU.mult))
            chain(v.tensor_scalar(turns, turns, ROUNDER, None, ALU.add))
            chain(v.tensor_scalar(turns, turns, ROUNDER, None, ALU.subtract))
            chain(v.scalar_tensor_tensor(out=r, in0=turns, scalar=-PI_A, in1=ang, op0=ALU.mult, op1=ALU.add))
            chain(v.scalar_tensor_tensor(out=ang, in0=turns, scalar=-PI_B, in1=r, op0=ALU.mult, op1=ALU.add))
            chain(v.scalar_tensor_tensor(out=r, in0=turns, scalar=-PI_C, in1=ang, op0=ALU.mult, op1=ALU.add))
            chain(v.tensor_scalar(sinT[:, :], r, PI_BELOW, -PI_BELOW, ALU.min, ALU.max))
            chain(v.scalar_tensor_tensor(out=rabs, in0=sinT[:, :], scalar=-1.0, in1=sinT[:, :], op0=ALU.mult, op1=ALU.max))
            v.tensor_scalar(cosT[:, :], rabs, -1.0, math.pi / 2, ALU.mult, ALU.add).then_inc(angles_ready, 1)
            lv = bufD[:, 3 * P:3 * P + 4 * DA_DIM].rearrange("p (n d) -> p n d", n=4)
            chain(v.tensor_tensor(bufD[:, 1024:1024 + DA_DIM], lv[:, 0, :], lv[:, 1, :], ALU.mult))
            chain(v.tensor_tensor(bufD[:, 1088:1088 + DA_DIM], lv[:, 2, :], lv[:, 3, :], ALU.mult))
            v.tensor_reduce(tiny[:, 0:2], bufD[:, 1024:1152].rearrange("p (n d) -> p n d", n=2), AX.X, ALU.add)\
                .then_inc(lam_dots, 1)

            def scale_x(n):
                wait_rstd()
                for t in range(TT):
                    v.tensor_scalar(C_tok[:, t, :], x[:, t, :], ss[:, t:t + 1], None, ALU.mult).then_inc(xn_ready, 1)

            def affine(n, bias_col, g_col, col_g):
                bank = dve_banks.take(dve)
                chain(v.tensor_tensor(mods[:, 0:16], bank[:, 0:16], col1[:, bias_col:bias_col + 16], ALU.add))
                chain(v.scalar_tensor_tensor(out=aff[:, :], in0=mods[:, 8:16], scalar=1.0, in1=col_g[:, g_col:g_col + 8],
                                             op0=ALU.add, op1=ALU.mult))
                dve.sem_inc(dve_freed, 1)
                dve.sem_inc(aff_ready, 1)

            def norm_evac():
                for k in range(1, KT, 2):
                    bank = dve_banks.take(dve)
                    v.tensor_scalar(hT[:, k, :], bank[:, :], aff[:, k:k + 1], mods[:, k:k + 1],
                                    ALU.mult, ALU.add).then_inc(dve_freed, 1)
                dve.wait_ge(dve_freed, dve_banks.n)
                dve.sem_inc(hT_dve, 4)

            def rope(raw, dst):
                bank = dve_banks.take(dve)
                a0 = steps(v.tensor_tensor(mix[:, 0, :], raw, cosT[:, :], ALU.mult))
                v.tensor_tensor(mix[:, 1, :], bank[:, :], sinT[:, :], ALU.mult).then_inc(dve_freed, 1)
                dve.wait_ge(dve_freed, dve_banks.n)
                steps.settle(a0)
                v.tensor_tensor(dst, mix[:, 0, :], mix[:, 1, :], ALU.add).then_inc(rope_ready, 1)
                ropes[0] += 1
                dve.wait_ge(rope_ready, ropes[0])

            ropes = [0]

            def gate_columns(n, bias_col):
                bank = dve_banks.take(dve)
                v.tensor_tensor(mods[:, 0:8], bank[:, 0:8], col1[:, bias_col:bias_col + 8], ALU.add).then_inc(dve_freed, 1)
                dve.wait_ge(dve_freed, dve_banks.n)
                for j in range(8):
                    last = v.tensor_scalar(gate_cols[:, j, :], ones, mods[:, j:j + 1], None, ALU.mult)
                last.then_inc(gatecols_ready, 1)

            def residual(n, count):
                dve.wait_ge(gate_ready, n + 1)
                for u in range(2):
                    for t in range(TT):
                        bank = dve_banks.take(dve)
                        j = (4 * u + t) % 2
                        v.tensor_tensor(mix[:, j, :], bank[:, :], gate_row[:, u * W:(u + 1) * W], ALU.mult).then_inc(dve_freed, 1)
                        dve.wait_ge(dve_freed, dve_banks.n)
                        xt = x[:, t, u * W:(u + 1) * W]
                        steps(v.tensor_tensor(xt, xt, mix[:, j, :], ALU.add))
                steps.settle()
                dve.sem_inc(x_ready, 1)

            def attention(base, splits, maxima, combine, post):
                n_steps = TT * HEADS

                def maxes(i):
                    banks = [act_banks.take(dve) for _ in range(splits)]
                    maxima(i, banks)

                maxes(0)
                for i in range(n_steps):
                    if i + 1 < n_steps:
                        maxes(i + 1)
                    if combine is not None:
                        combine(i)
                    if i >= 2:
                        post(i - 2)
                post(n_steps - 2)
                post(n_steps - 1)

            def skip(n):
                act_banks.n += n

            dve.wait_ge(lam_exps, 1)
            chain(v.tensor_tensor(lam[:, 2:3], lam[:, 1:2], lam[:, 0:1], ALU.subtract))
            chain(v.tensor_scalar(lam[:, 3:4], lam[:, 2:3], -LAMBDA_INIT, None, ALU.add))
            scale_x(0)
            affine(0, R1["ada_b0"], R1["norm_g0"], col1)
            norm_evac()
            dve.wait_ge(sincos_ready, 1)
            for f in range(16):
                if f == 15:
                    bank = dve_banks.take(dve)
                    v.tensor_copy(C_tok[:, 0, 0:W], bank[:, :]).then_inc(dve_freed, 1)
                    dve.wait_ge(dve_freed, dve_banks.n)
                    dve.sem_inc(v_ready, 1)
                rope(probs[:, f % 3, :], A8[:, f, :] if f < 8 else B8[:, f - 8, :])
            for u in range(2):
                for t in range(TT):
                    if u == 0 and t == 0:
                        continue
                    bank = dve_banks.take(dve)
                    v.tensor_copy(C_tok[:, t, u * W:(u + 1) * W], bank[:, :]).then_inc(dve_freed, 1)
                    dve.wait_ge(dve_freed, dve_banks.n)
                    dve.sem_inc(v_ready, 1)
            skip(3 + 4 + 16 + 8)

            def maxima0(i, banks):
                c = 2 * i
                for s, bank in enumerate(banks):
                    last = steps(v.tensor_reduce(negmax[:, c + s:c + s + 1], bank[:, :], AX.X, ALU.max, negate=True))
                steps.settle()
                dve.sem_inc(max_ready, 1)

            def combine0(i):
                c = 2 * i
                dve.wait_ge(exp_ready, i + 1)
                chain(v.reciprocal(inv_sums[:, c:c + 2], sums[:, c:c + 2]))
                chain(v.scalar_tensor_tensor(out=inv_sums[:, c + 1:c + 2], in0=inv_sums[:, c + 1:c + 2], scalar=lam[:, 3:4],
                                             in1=sums[:, c:c + 1], op0=ALU.mult, op1=ALU.mult))
                p1, p2 = probs[:, 2 * (i % 2), :], probs[:, 2 * (i % 2) + 1, :]
                v.scalar_tensor_tensor(out=mix[:, i % 3, :], in0=p2, scalar=inv_sums[:, c + 1:c + 2], in1=p1,
                                       op0=ALU.mult, op1=ALU.add).then_inc(mix_ready, 1)

            def post0(i):
                t, h = i // HEADS, i % HEADS
                bank = dve_banks.take(dve)
                v.tensor_scalar(o_raw[:, t, h * P:(h + 1) * P], bank[:, 0:P], inv_sums[:, 2 * i:2 * i + 1], None,
                                ALU.mult).then_inc(dve_freed, 1)
                if h == 1 and t > 0:
                    finish_heads(t - 1)
                if h == HEADS - 1:
                    dve.wait_ge(dve_freed, dve_banks.n)
                    sq = bufE[:, 0:D]
                    chain(v.tensor_tensor(sq, o_raw[:, t, :], o_raw[:, t, :], ALU.mult))
                    v.tensor_reduce(ss[:, 0:8], sq.rearrange("p (h d) -> p h d", h=HEADS), AX.X, ALU.add)\
                        .then_inc(squares_ready, 1)
                    if t == TT - 1:
                        finish_heads(t)

            def finish_heads(t):
                wait_rstd()
                for h in range(HEADS):
                    zt = D_tok[:, t, h * P:(h + 1) * P]
                    steps(v.scalar_tensor_tensor(out=zt, in0=o_raw[:, t, h * P:(h + 1) * P], scalar=ss[:, h:h + 1],
                                                 in1=zt, op0=ALU.mult, op1=ALU.mult))
                steps.settle()
                dve.sem_inc(og_ready, 1)

            dve.wait_ge(z_ready, 1)
            attention(0, 2, maxima0, combine0, post0)
            gate_columns(0, R1["ada_b0"] + 16)
            skip(2)
            residual(0, 0)

            scale_x(1)
            affine(1, R1["ada_b1"], R1["norm_g1"], col1)
            norm_evac()
            skip(4 + 16)
            dve.wait_ge(raw1_ready, 1)
            latents = tok(bufA, 768)
            for t in range(TT):
                for n, (lo, hi) in enumerate(((0, Q_LORA), (Q_LORA, Q_LORA + KV_LORA))):
                    part = latents[:, t, lo:hi]
                    chain(v.tensor_tensor(mix[:, n, 0:hi - lo], part, part, ALU.mult))
                    chain(v.tensor_reduce(ss[:, 4 * n + t:4 * n + t + 1], mix[:, n, 0:hi - lo], AX.X, ALU.add))
            chain(v.tensor_scalar(ss[:, 0:4], ss[:, 0:4], 1.0 / Q_LORA, None, ALU.mult))
            v.tensor_scalar(ss[:, 4:8], ss[:, 4:8], 1.0 / KV_LORA, None, ALU.mult).then_inc(squares_ready, 1)
            wait_rstd()
            for t in range(TT):
                steps(v.tensor_copy(latents[:, t, 704:768], latents[:, t, 640:704]))
                for n, (lo, hi) in enumerate(((0, Q_LORA), (Q_LORA, Q_LORA + KV_LORA))):
                    part = latents[:, t, lo:hi]
                    steps(v.tensor_scalar(part, part, ss[:, 4 * n + t:4 * n + t + 1], None, ALU.mult))
            steps.settle()
            dve.sem_inc(n1_ready, TT)
            E5 = feat(bufE, 5)
            rope(B8[:, 5, :], E5[:, 4, :])
            for pair in range(4):
                rope(probs[:, pair % 3, :], E5[:, pair, :])
            for nb in range(2):
                for t in range(TT):
                    bank = dve_banks.take(dve)
                    v.tensor_copy(C_tok[:, t, nb * W:(nb + 1) * W], bank[:, :]).then_inc(dve_freed, 1)
                    dve.wait_ge(dve_freed, dve_banks.n)
                    dve.sem_inc(v_ready, 1)
            skip(12 + 8)
            dve.wait_ge(z_ready, 2)

            def maxima1(i, banks):
                chain(v.tensor_reduce(negmax[:, i:i + 1], banks[0][:, :], AX.X, ALU.max, negate=True))
                v.tensor_scalar(negmax[:, i:i + 1], negmax[:, i:i + 1], MLA_SCALE, None, ALU.mult).then_inc(max_ready, 1)

            def post1(i):
                t, h = i // HEADS, i % HEADS
                chain(v.reciprocal(inv_sums[:, i:i + 1], sums[:, i:i + 1]))
                bank = dve_banks.take(dve)
                zt = D_tok[:, t, h * P:(h + 1) * P]
                v.scalar_tensor_tensor(out=zt, in0=bank[:, 0:P], scalar=inv_sums[:, i:i + 1], in1=zt,
                                       op0=ALU.mult, op1=ALU.mult).then_inc(dve_freed, 1)
                if h == HEADS - 1:
                    dve.wait_ge(dve_freed, dve_banks.n)
                    dve.sem_inc(og_ready, 1)

            def post_with_exp(base, post):
                def run(i):
                    dve.wait_ge(exp_ready, base + i + 1)
                    post(i)
                return run

            attention(32, 1, maxima1, None, post_with_exp(32, post1))
            gate_columns(1, R1["ada_b1"] + 16)
            skip(2)
            residual(1, 1)
            wait_rstd()
            dve.wait_ge(norm_row_in, 16)
            for t in range(TT):
                steps(v.scalar_tensor_tensor(out=x[:, t, :], in0=x[:, t, :], scalar=ss[:, t:t + 1], in1=norm_row[:, :],
                                             op0=ALU.mult, op1=ALU.mult))
            steps.settle()
            dve.sem_inc(norm_row_used, 1)
            dve.sem_inc(x_ready, 1)

            scale_x(2)
            affine(2, R1["b_mod"], R1["g_norm1"], col1)
            norm_evac()
            skip(4 + 4 + 12)
            U = bufC[:, 0:CH * (T + PAD)].rearrange("p (c n) -> p c n", c=CH)
            conv = feat(bufD, CH, 2048)
            for j in range(CH):
                bank = dve_banks.take(dve)
                if j == 0:
                    steps(v.memset(U[:, :, 0:PAD], 0.0))
                dve.wait_ge(sig_ready, j + 1)
                v.tensor_tensor(U[:, j, PAD:PAD + T], bank[:, :], mix[:, j % 2, :], ALU.mult).then_inc(dve_freed, 1)
                dve.wait_ge(dve_freed, dve_banks.n)
                dve.sem_inc(u_used, 1)
            steps.settle()
            for tap in range(TAPS):
                for j in range(CH):
                    wcol = col3[:, tap * CH + j:tap * CH + j + 1]
                    src = U[:, j, tap:tap + T]
                    if tap == 0:
                        steps(v.tensor_scalar(conv[:, j, :], src, wcol, col2[:, R2["conv_b"] + j:R2["conv_b"] + j + 1],
                                              ALU.mult, ALU.add))
                    else:
                        steps.settle(steps.n - CH + 1)
                        steps(v.scalar_tensor_tensor(out=conv[:, j, :], in0=src, scalar=wcol, in1=conv[:, j, :],
                                                     op0=ALU.mult, op1=ALU.add))
            steps.settle()
            dve.sem_inc(conv_ready, CH)
            lnorm = tok(bufC, W)
            for t in range(TT):
                bank = dve_banks.take(dve)
                chain(v.tensor_reduce(tiny[:, 8 + t:9 + t], bank[:, :], AX.X, ALU.add))
                chain(v.tensor_scalar(tiny[:, 8 + t:9 + t], tiny[:, 8 + t:9 + t], -1.0 / W, None, ALU.mult))
                v.tensor_scalar(lnorm[:, t, :], bank[:, :], tiny[:, 8 + t:9 + t], None, ALU.add).then_inc(dve_freed, 1)
                dve.wait_ge(dve_freed, dve_banks.n)
                chain(v.tensor_tensor(mix[:, 0, :], lnorm[:, t, :], lnorm[:, t, :], ALU.mult))
                chain(v.tensor_reduce(ss[:, t:t + 1], mix[:, 0, :], AX.X, ALU.add))
            dve.sem_inc(squares_ready, 1)
            wait_rstd()
            for t in range(TT):
                v.tensor_scalar(lnorm[:, t, :], lnorm[:, t, :], ss[:, t:t + 1], None, ALU.mult).then_inc(ln_ready, 1)
            dve.wait_ge(alibi_in, 16)
            alibi = feat(bufB)

            def maxima2(i, banks):
                t, h = i // HEADS, i % HEADS
                n = P * (t + 1)
                chain(v.tensor_tensor(banks[0][:, 0:n], banks[0][:, 0:n], alibi[:, h, T - n:T], ALU.add))
                v.tensor_reduce(negmax[:, i:i + 1], banks[0][:, 0:n], AX.X, ALU.max, negate=True).then_inc(max_ready, 1)

            attn2 = tok(bufD, W)

            def post2(i):
                t, h = i // HEADS, i % HEADS
                chain(v.reciprocal(inv_sums[:, i:i + 1], sums[:, i:i + 1]))
                bank = dve_banks.take(dve)
                v.tensor_scalar(attn2[:, t, h * ALIBI_DIM:(h + 1) * ALIBI_DIM], bank[:, 0:ALIBI_DIM],
                                inv_sums[:, i:i + 1], None, ALU.mult).then_inc(dve_freed, 1)
                if h == HEADS - 1:
                    dve.wait_ge(dve_freed, dve_banks.n)
                    dve.sem_inc(og_ready, 1)

            attention(64, 1, maxima2, None, post_with_exp(64, post2))
            gate_columns(2, R1["b_mod"] + 16)
            skip(2)
            residual(2, 3)

            scale_x(3)
            affine(3, R1["b_mod"] + 24, R2["g_norm2"], col2)
            norm_evac()
            chain(v.tensor_copy(shift2[:, :], mods[:, 0:8]))
            route()
            gate_columns(3, R1["b_mod"] + 40)

            def flip(p, n, first=False):
                dve.wait_ge(xg_read, n + 1)
                if not first:
                    dve.wait_ge(up_done, n - 1)
                    dve.wait_ge(xgT_ready, n)
                shift_b = shift2[:, :].unsqueeze(2).to_broadcast([P, KT, SLOTS])
                for b in range(2):
                    ks = slice(b * BANK_K, (b + 1) * BANK_K)
                    v.tensor_tensor(xg_t[:, ks, :], psum[b][:, :].rearrange("p (k s) -> p k s", k=BANK_K),
                                    aff[:, ks].unsqueeze(2).to_broadcast([P, BANK_K, SLOTS]), ALU.mult).then_inc(xg_scaled, 1)
                dve.wait_ge(xg_scaled, 2 * n + 2)
                v.tensor_tensor(xgT[p], xg_t, shift_b, ALU.add).then_inc(xgT_ready, 1)

            def swiglu(p, n, first=False):
                dve.wait_ge(sg_ready, n + 1)
                dve.wait_ge(up_done, n + 1)
                if not first:
                    dve.wait_ge(down_done, n - 1)
                v.tensor_tensor(hTe[p], sg[p].rearrange("p (f s) -> p f s", f=FT),
                                psum[3][:, 0:FT * SLOTS].rearrange("p (f s) -> p f s", f=FT), ALU.mult).then_inc(h_ready, 1)

            flip(0, 0, first=True)
            swiglu(0, 0, first=True)
            dve.wait_ge(xgT_ready, 1)
            flip(1, 1, first=True)
            swiglu(1, 1, first=True)
            flip(0, 2)
            with dve.Fori(1, EXPERTS // 2 - 1) as i:
                swiglu(0, 2 * i)
                flip(1, 2 * i + 1)
                swiglu(1, 2 * i + 1)
                flip(0, 2 * i + 2)
            swiglu(0, EXPERTS - 2)
            flip(1, EXPERTS - 1)
            swiglu(1, EXPERTS - 1)
            n_over = dve.value_load(over_ids[0:1, OVER:OVER + 1], min_val=0, max_val=OVER)
            with dve.If(n_over > 0), dve.Fori(0, n_over) as k:
                flip(0, EXPERTS + k)
                swiglu(0, EXPERTS + k)
            dve.wait_ge(gate_ready, 4)
            for t in range(TT):
                dve.wait_ge(gath[t], 32)
                dve.wait_ge(weighted, t + 1)
                y0, y1 = ring[0][:, t * D:(t + 1) * D], ring[1][:, t * D:(t + 1) * D]
                chain(v.scalar_tensor_tensor(out=y0, in0=y1, scalar=wts[:, 1, t:t + 1], in1=y0, op0=ALU.mult, op1=ALU.add))
                chain(v.tensor_tensor(y0, y0, gate_row[:, :], ALU.mult))
                chain(v.tensor_tensor(x[:, t, :], x[:, t, :], y0, ALU.add))
                dve.sem_inc(x_ready, 1)
            wait_rstd()
            dve.wait_ge(norm_row_in, 32)
            for t in range(TT):
                v.scalar_tensor_tensor(out=bufA[:, t * D:(t + 1) * D], in0=x[:, t, :], scalar=ss[:, t:t + 1],
                                       in1=norm_row[:, :], op0=ALU.mult, op1=ALU.mult).then_inc(prod_ready, 1)


def constants():
    k = np.zeros((P, K_COLS), np.float32)
    k[:, K_IDENT:K_IDENT + P] = np.eye(P)
    half = ROPE // 2
    for m in range(P):
        if m % ROPE < half:
            k[m + half, K_ROT + m] = -1.0
        else:
            k[m - half, K_ROT + m] = 1.0
    k[:, K_UPPER:K_UPPER + P] = np.triu(np.ones((P, P)), 1)
    k[:, K_ONES:K_ONES + P] = 1.0
    inv = np.array([10000.0 ** (-i / half) for i in range(half)]).astype(np.float32)
    k[:, K_INV] = np.tile(inv, P // half)
    k[:, K_IOTA4:K_IOTA4 + GROUPS] = np.arange(GROUPS)
    k[:, K_IOTA32:K_IOTA32 + EXPERTS] = np.arange(EXPERTS)
    k[:, K_ITEM:K_ITEM + OVER] = np.arange(OVER)
    return k


def alibi_table():
    q = np.arange(P)[:, None]
    dist = q - (np.arange(T)[None, :] - (T - P))
    windows = np.zeros((P, T))
    for window, dil in ((128, 1), (512, 4), (2048, 16)):
        windows += (dist >= 0) & (dist <= window) & (dist % dil == 0)
    count = np.where(windows > 0, np.log(np.maximum(windows, 1)), NEG)
    slopes = 2.0 ** (-8.0 * np.arange(1, HEADS + 1) / HEADS)
    table = np.where(windows[:, None, :] > 0, -slopes[None, :, None] * dist[:, None, :] + count[:, None, :], NEG)
    return np.ascontiguousarray(table.reshape(P, HEADS * T).astype(np.float32))


_INS = ["x", "c", "positions", "ada_w0", "ada_b0", "norm_g0", "w_in0", "lam_q1", "lam_k1", "lam_q2", "lam_k2", "subln_g",
        "w_out0", "ada_w1", "ada_b1", "norm_g1", "w_in1", "q_a_norm_g", "w_q_b", "kv_a_norm_g", "w_kv_b", "w_out1",
        "final_norm_g", "c_2", "w_mod_2", "b_mod_2", "g_norm1_2", "w_in_2", "conv_w_2", "conv_b_2", "conv_ln_g_2",
        "conv_ln_b_2", "w_out_2", "g_norm2_2", "w_router_group_2", "b_router_group_2", "w_router_expert_2",
        "b_router_expert_2", "w_exp_gate_2", "w_exp_up_2", "w_exp_down_2", "g_final_2"]


def kernel(**inputs):
    import concourse.bacc as bacc
    from concourse.bass_utils import run_bass_kernel_spmd

    nc = bacc.Bacc("TRN2", target_bir_lowering=False, num_devices=1)
    arrays, aps = {}, {}
    given = {name: np.ascontiguousarray(inputs[name]) for name in _INS}
    given["constants"] = constants()
    given["alibi"] = alibi_table()
    for name, value in given.items():
        arrays[f"in_{name}"] = value
        aps[name] = nc.dram_tensor(f"in_{name}", value.shape, mybir.dt.from_np(value.dtype), kind="ExternalInput").ap()
    out = nc.dram_tensor("out_0", (1, T, D), F32, kind="ExternalOutput").ap()
    xs = nc.dram_tensor("expert_rows", (ITEMS * SLOTS, D), F32, kind="Internal").ap()
    ys = nc.dram_tensor("expert_results", (ITEMS * SLOTS, D), F32, kind="Internal").ap()
    fused_kernel(nc, aps, out, xs, ys)
    r = run_bass_kernel_spmd(nc, [arrays], core_ids=[0])
    return r.results[0]["out_0"]
```
